# Optimizing a Trainium2 kernel written in Bass

```python
import math
import jax, jax.numpy as jnp
from jax import lax
import numpy as np

D_MODEL = 1024
BATCH = 1
SEQ = 512
DEPTH = 1
DEC_BATCH = 1
DEC_SEQ = 2048
PAST_LEN = 128

D_PLE = 256
RW_HEADS = 8
RW_HEAD_DIM = 64
RW_WIDTH = RW_HEADS * RW_HEAD_DIM
W_LORA = 64
A_LORA = 64
RW_CONV_COLS = 3 * RW_WIDTH + 2 * W_LORA + A_LORA
DA_HEADS = 4
DA_QK_DIM = 64
DA_V_DIM = 2 * DA_QK_DIM
DA_WIDTH = DA_HEADS * DA_V_DIM
MIX_WIDTH = RW_WIDTH + DA_WIDTH
IN_COLS = RW_CONV_COLS + RW_WIDTH + 4 * DA_WIDTH
CONV_WIDTH = 3
Q_BLOCK = 128
NORM_EPS = 1e-6
LN_X_EPS = 64e-5
KK_EPS = 1e-12
ALIBI_MAX_BIAS = 8.0

kernel_name = 'hybrid_rwkv7_diffattn_encoder'

def rmsnorm(x, g, eps=NORM_EPS):
    xf = x.astype(jnp.float32)
    y = xf * lax.rsqrt(jnp.mean(xf * xf, axis=-1, keepdims=True) + eps)
    return (y * g.astype(jnp.float32)).astype(x.dtype)

def centred_conv(x, w, b):
    pad = CONV_WIDTH // 2
    S = x.shape[1]
    xp = jnp.pad(x, ((0, 0), (pad, pad), (0, 0)))
    out = b
    for i in range(CONV_WIDTH):
        out = out + xp[:, i:i + S] * w[i]
    return out

def both_dirs(t):
    tm = jnp.moveaxis(t, 1, 0)
    return jnp.stack([tm, tm[::-1]], axis=1)

def rwkv7_mixer(c, w0, w_up, a0, a_up, k_k, k_a, r_k, ln_g, ln_b):
    f32 = jnp.float32
    B, S, _ = c.shape
    H, N = RW_HEADS, RW_HEAD_DIM
    o = 3 * RW_WIDTH
    r = c[..., :RW_WIDTH].astype(f32).reshape(B, S, H, N)
    k = c[..., RW_WIDTH:2 * RW_WIDTH].astype(f32).reshape(B, S, H, N)
    v = c[..., 2 * RW_WIDTH:o].astype(f32).reshape(B, S, H, N)
    zw = c[..., o:o + 2 * W_LORA].astype(f32).reshape(B, S, 2, W_LORA)
    za = c[..., o + 2 * W_LORA:].astype(f32)
    w_logit = w0.astype(f32) + jnp.einsum('bsdr,drc->bsdc', jnp.tanh(zw), w_up.astype(f32))
    decay = jnp.exp(-jnp.exp(-jax.nn.softplus(-w_logit) - 0.5)).reshape(B, S, 2, H, N)
    a = jax.nn.sigmoid(a0.astype(f32) + za @ a_up.astype(f32)).reshape(B, S, H, N)
    kk = k * k_k.astype(f32).reshape(H, N)
    kk = kk * lax.rsqrt(jnp.sum(kk * kk, axis=-1, keepdims=True) + KK_EPS)
    k = k * (1.0 + (a - 1.0) * k_a.astype(f32).reshape(H, N))
    dtm = jnp.moveaxis(decay, 1, 0)
    w_s = jnp.stack([dtm[:, :, 0], dtm[::-1, :, 1]], axis=1)
    xs = (both_dirs(r), w_s, both_dirs(k), both_dirs(v), both_dirs(-kk), both_dirs(kk * a))

    def step(state, inp):
        r_t, w_t, k_t, v_t, a_t, b_t = inp
        sa = jnp.einsum('dbhij,dbhj->dbhi', state, a_t)
        state = (state * w_t[..., None, :] + sa[..., :, None] * b_t[..., None, :]
                 + v_t[..., :, None] * k_t[..., None, :])
        y_t = jnp.einsum('dbhij,dbhj->dbhi', state, r_t)
        return state, y_t

    state0 = jnp.zeros((2, B, H, N, N), f32)
    _, ys = lax.scan(step, state0, xs)
    y = jnp.moveaxis(ys[:, 0] + ys[::-1, 1], 0, 1)
    mu = jnp.mean(y, axis=-1, keepdims=True)
    var = jnp.mean(jnp.square(y - mu), axis=-1, keepdims=True)
    y = ((y - mu) * lax.rsqrt(var + LN_X_EPS) * ln_g.astype(f32).reshape(H, N)
         + ln_b.astype(f32).reshape(H, N))
    bonus = jnp.sum(r * k * r_k.astype(f32), axis=-1, keepdims=True) * v
    return (y + bonus).reshape(B, S, RW_WIDTH)

def diff_attention_mixer(q, k, v, q_norm, k_norm, lam_vec, subln, lam_init):
    f32 = jnp.float32
    B, S, _ = q.shape
    H, d, dv = DA_HEADS, DA_QK_DIM, DA_V_DIM
    q = rmsnorm(q.reshape(B, S, H, 2, d), q_norm) * (d ** -0.5)
    k = rmsnorm(k.reshape(B, S, H, 2, d), k_norm)
    v = v.reshape(B, S, H, dv)
    lv = lam_vec.astype(f32)
    lam = jnp.exp(jnp.sum(lv[0] * lv[1])) - jnp.exp(jnp.sum(lv[2] * lv[3])) + lam_init
    slopes = 2.0 ** (-ALIBI_MAX_BIAS * jnp.arange(1, H + 1, dtype=f32) / H)
    nb = S // Q_BLOCK
    q_blocks = jnp.moveaxis(q.reshape(B, nb, Q_BLOCK, H, 2, d), 1, 0)
    starts = jnp.arange(nb, dtype=jnp.int32) * Q_BLOCK
    kpos = jnp.arange(S, dtype=jnp.int32)

    def attend(args):
        qb, q0 = args
        s = jnp.einsum('bqhmd,bkhmd->bhmqk', qb, k, preferred_element_type=f32)
        qpos = q0 + jnp.arange(Q_BLOCK, dtype=jnp.int32)
        dist = jnp.abs(qpos[:, None] - kpos[None, :]).astype(f32)
        s = s - slopes[None, :, None, None, None] * dist
        pr = jax.nn.softmax(s, axis=-1)
        att = pr[:, :, 0] - lam * pr[:, :, 1]
        return jnp.einsum('bhqk,bkhe->bqhe', att.astype(v.dtype), v)

    o = lax.map(attend, (q_blocks, starts))
    o = jnp.moveaxis(o, 0, 1).reshape(B, S, H, dv)
    o = rmsnorm(o, subln) * (1.0 - lam_init)
    return o.reshape(B, S, DA_WIDTH)

def hybrid_layer(h, p_i, lam_init, prm):
    u = rmsnorm(h, prm['norm_pre'])
    proj = u @ prm['w_in']
    o0 = RW_CONV_COLS
    o1 = o0 + RW_WIDTH
    o2 = o1 + DA_WIDTH
    o3 = o2 + DA_WIDTH
    o4 = o3 + DA_WIDTH
    c = centred_conv(proj[..., :o0], prm['rw_conv_w'], prm['rw_conv_b'])
    y_rw = rwkv7_mixer(c, prm['rw_w0'], prm['rw_w_up'], prm['rw_a0'], prm['rw_a_up'],
                       prm['rw_k_k'], prm['rw_k_a'], prm['rw_r_k'], prm['rw_ln_g'], prm['rw_ln_b'])
    y_rw = y_rw.astype(h.dtype) * jax.nn.silu(proj[..., o0:o1])
    y_da = diff_attention_mixer(proj[..., o1:o2], proj[..., o2:o3], proj[..., o3:o4],
                                prm['da_q_norm'], prm['da_k_norm'], prm['da_lambda'],
                                prm['da_subln'], lam_init)
    y_da = y_da.astype(h.dtype) * jax.nn.silu(proj[..., o4:])
    h = h + jnp.concatenate([y_rw, y_da], axis=-1) @ prm['w_out']
    e = rmsnorm(p_i @ prm['ple_proj'], prm['ple_norm'])
    gate = jax.nn.sigmoid(h @ prm['ple_gate_w'] + prm['ple_gate_b'])
    return h + gate * e

def run_trunk(x, p, params):
    h = x
    for i in range(DEPTH):
        prm = {name: arr[i] for name, arr in params.items()}
        lam_init = 0.8 - 0.6 * math.exp(-0.3 * i)
        h = hybrid_layer(h, p[i], lam_init, prm)
    return h

def setup_inputs(seed: int = 0) -> dict:
    key = jax.random.key(seed)
    ks = jax.random.split(key, 32)
    f32 = jnp.float32

    def nrm(k, shape, s):
        return s * jax.random.normal(k, shape, f32)

    return {
        'x_prompt': nrm(ks[0], (BATCH, SEQ, D_MODEL), 1.0),
        'x_sample': nrm(ks[1], (DEC_BATCH, DEC_SEQ, D_MODEL), 1.0),
        'p_prompt': nrm(ks[2], (DEPTH, BATCH, SEQ, D_PLE), 1.0),
        'p_sample': nrm(ks[3], (DEPTH, DEC_BATCH, DEC_SEQ, D_PLE), 1.0),
        'norm_pre': 1.0 + nrm(ks[4], (DEPTH, D_MODEL), 0.05),
        'w_in': nrm(ks[5], (DEPTH, D_MODEL, IN_COLS), D_MODEL ** -0.5),
        'w_out': nrm(ks[6], (DEPTH, MIX_WIDTH, D_MODEL), MIX_WIDTH ** -0.5),
        'rw_conv_w': jnp.array([0.25, 1.0, 0.25], f32)[None, :, None]
                     + nrm(ks[7], (DEPTH, CONV_WIDTH, RW_CONV_COLS), 0.05),
        'rw_conv_b': nrm(ks[8], (DEPTH, RW_CONV_COLS), 0.01),
        'rw_w0': nrm(ks[9], (DEPTH, 2, RW_WIDTH), 1.0) - 0.5,
        'rw_w_up': nrm(ks[10], (DEPTH, 2, W_LORA, RW_WIDTH), 0.5 * W_LORA ** -0.5),
        'rw_a0': nrm(ks[11], (DEPTH, RW_WIDTH), 0.1),
        'rw_a_up': nrm(ks[12], (DEPTH, A_LORA, RW_WIDTH), 0.5 * A_LORA ** -0.5),
        'rw_k_k': 0.85 + nrm(ks[13], (DEPTH, RW_WIDTH), 0.05),
        'rw_k_a': 1.0 + nrm(ks[14], (DEPTH, RW_WIDTH), 0.05),
        'rw_r_k': nrm(ks[15], (DEPTH, RW_HEADS, RW_HEAD_DIM), 0.1),
        'rw_ln_g': 1.0 + nrm(ks[16], (DEPTH, RW_WIDTH), 0.05),
        'rw_ln_b': nrm(ks[17], (DEPTH, RW_WIDTH), 0.01),
        'da_q_norm': 1.0 + nrm(ks[18], (DEPTH, 2, DA_QK_DIM), 0.05),
        'da_k_norm': 1.0 + nrm(ks[19], (DEPTH, 2, DA_QK_DIM), 0.05),
        'da_lambda': nrm(ks[20], (DEPTH, 4, DA_QK_DIM), 0.1),
        'da_subln': 1.0 + nrm(ks[21], (DEPTH, DA_V_DIM), 0.05),
        'ple_proj': nrm(ks[22], (DEPTH, D_PLE, D_MODEL), D_PLE ** -0.5),
        'ple_norm': 1.0 + nrm(ks[23], (DEPTH, D_MODEL), 0.05),
        'ple_gate_w': nrm(ks[24], (DEPTH, D_MODEL, D_MODEL), D_MODEL ** -0.5),
        'ple_gate_b': nrm(ks[25], (DEPTH, D_MODEL), 0.01),
    }

def reference(x_prompt, x_sample, p_prompt, p_sample, norm_pre, w_in, w_out,
              rw_conv_w, rw_conv_b, rw_w0, rw_w_up, rw_a0, rw_a_up, rw_k_k, rw_k_a, rw_r_k,
              rw_ln_g, rw_ln_b, da_q_norm, da_k_norm, da_lambda, da_subln,
              ple_proj, ple_norm, ple_gate_w, ple_gate_b):
    params = dict(norm_pre=norm_pre, w_in=w_in, w_out=w_out,
                  rw_conv_w=rw_conv_w, rw_conv_b=rw_conv_b, rw_w0=rw_w0, rw_w_up=rw_w_up,
                  rw_a0=rw_a0, rw_a_up=rw_a_up, rw_k_k=rw_k_k, rw_k_a=rw_k_a, rw_r_k=rw_r_k,
                  rw_ln_g=rw_ln_g, rw_ln_b=rw_ln_b, da_q_norm=da_q_norm, da_k_norm=da_k_norm,
                  da_lambda=da_lambda, da_subln=da_subln, ple_proj=ple_proj, ple_norm=ple_norm,
                  ple_gate_w=ple_gate_w, ple_gate_b=ple_gate_b)
    y_prompt = run_trunk(x_prompt, p_prompt, params)
    y_sample = run_trunk(x_sample, p_sample, params)
    return (y_prompt, y_sample)


_drawn_inputs = setup_inputs


def setup_inputs(seed=0):
    import zlib

    import numpy as np

    out = dict(_drawn_inputs(seed))
    spreads = {}
    factors = {'rw_conv_b': 8.0,
     'rw_a0': 3.01,
     'rw_k_k': 43.654,
     'rw_ln_g': 3.323,
     'rw_ln_b': 35.426,
     'da_q_norm': 4.342,
     'da_k_norm': 4.274,
     'da_subln': 4.184,
     'ple_norm': 2.705,
     'ple_gate_b': 35.044}
    for name, (base, spread) in spreads.items():
        noise = np.random.default_rng([zlib.crc32(name.encode()), seed]).standard_normal(out[name].shape)
        drawn = base * np.exp(spread * noise) if base else spread * noise
        out[name] = __import__('jax').numpy.asarray(drawn.astype(out[name].dtype))
    for name, factor in factors.items():
        out[name] = (out[name] * factor).astype(out[name].dtype)
    return out
```

```python
import concourse.bass as bass
from concourse import mybir
from contextlib import ExitStack

F32 = mybir.dt.float32
ALU = mybir.AluOpType
ACT = mybir.ActivationFunctionType
AX = mybir.AxisListType

D_MODEL = 1024
D_PLE = 256
RW_HEADS, RW_DIM = 8, 64
RW_WIDTH = RW_HEADS * RW_DIM
LORA = 64
CONV_COLS = 3 * RW_WIDTH + 3 * LORA
DA_HEADS, DA_DIM = 4, 64
DA_WIDTH = DA_HEADS * 2 * DA_DIM
IN_COLS = CONV_COLS + RW_WIDTH + 4 * DA_WIDTH
P = 128
KC = D_MODEL // P
LAM_INIT = 0.8 - 0.6
NORM_EPS, LN_EPS, KK_EPS = 1e-6, 64e-5, 1e-12
W_SCALE = 0.6065306597126334
SLOPES = [2.0 ** (-8.0 * (h + 1) / DA_HEADS) for h in range(DA_HEADS)]


class Phase:

    def __init__(self, nc, name):
        self.nc, self.name, self.ctx, self.sems = nc, name, ExitStack(), []

    def __enter__(self):
        self.ctx.__enter__()
        return self

    def __exit__(self, *e):
        self.ctx.__exit__(*e)
        self.nc.clear_and_free_semaphores(self.sems)
        self.nc.all_engine_barrier()

    def sb(self, name, shape):
        return self.ctx.enter_context(self.nc.sbuf_tensor(f"{self.name}_{name}", shape, F32))

    def banks(self, name, n):
        return [self.ctx.enter_context(self.nc.psum_tensor(f"{self.name}_{name}{i}", [P, 512], F32)) for i in range(n)]

    def sem(self, name):
        self.sems.append(self.nc.alloc_semaphore(f"{self.name}_{name}"))
        return self.sems[-1]


class Steps:

    def __init__(self, eng, sem, base):
        self.eng, self.sem, self.base, self.n = eng, sem, base, 0

    def step(self, instruction):
        instruction.then_inc(self.sem, 1)
        self.n += 1

    def settle(self):
        self.eng.wait_ge(self.sem, self.base + self.n)


def project_phase(nc, tokens, x_blocks, norm_pre, w_in, q_gain, k_gain, ident_d, conv_in, q_kT, v_tok, gates):
    BT = 256
    NB = tokens // BT
    NM = (CONV_COLS + P - 1) // P
    LAST = CONV_COLS - (NM - 1) * P
    with Phase(nc, "pj") as ph:
        w = ph.sb("w", [P, KC, IN_COLS])
        x = ph.sb("x", [P, 2, D_MODEL])
        uT = [ph.sb(f"uT{i}", [P, KC, BT]) for i in range(2)]
        conv_out = ph.sb("conv_out", [P, NM, BT])
        tok_out = ph.sb("tok_out", [P, 3, 2, 512])
        qk_out = ph.sb("qk_out", [P, 2, 4, BT])
        qk = ph.sb("qk", [P, 1024])
        junk = ph.sb("junk", [P, 1024])
        qk_gain = ph.sb("qk_gain", [P, 1024])
        ident = ph.sb("ident", [P, P])
        gain = ph.sb("gain", [P, KC])
        xs = ph.sb("xs", [P, 2, 3])
        qs = ph.sb("qs", [P, 3, 16])
        tr = ph.banks("tr", 2)
        cm = ph.banks("cm", 2)
        tm = ph.banks("tm", 4)
        s = {n: ph.sem(n) for n in (
            "w0", "w1", "w2", "w3", "const", "gain_q", "x_loaded", "x_squared", "x_mean", "x_root", "x_step", "xn_ready", "tr_ready",
            "tr_evac", "cm_ready", "cm_evac", "tm_ready", "tm_act", "tm_dve", "qk_squared", "qk_mean",
            "qk_root", "qk_step", "qkn_ready", "conv_stored", "tok_stored", "qk_stored", "passed")}
        CUTS = [0, 896, CONV_COLS, CONV_COLS + 3 * 512, IN_COLS]
        O = CONV_COLS
        TOK_COLS = [O + 512, O + 1024, O + 1536, O, O + 2048]
        w_v = w_in.rearrange("(k p) n -> p k n", p=P)
        conv_v = conv_in[:, 1:1 + tokens].rearrange("(m p) (b t) -> b p m t", p=P, t=BT)
        v_v = v_tok.rearrange("(b t p) c -> b p t c", t=2, p=P)
        g_v = [gates[i].rearrange("(b t p) c -> b p t c", t=2, p=P) for i in range(2)]
        qk_v = q_kT.rearrange("(q h p) (b t) -> b q p h t", q=2, p=P, t=BT)
        block = ph.ctx.enter_context(nc.Block())

        def blocks(eng, body, **kw):
            with eng.Fori(0, NB // 2 - 1) as j:
                body(j * 2, 0, True)
                body(j * 2 + 1, 1, True)
            body(NB - 2, 0, True)
            body(NB - 1, 1, False)

        @block.sync
        def _(sp):
            sp.dma_start(x[:, :, :], x_blocks[0]).then_inc(s["x_loaded"], 16)
            sp.dma_start(ident[:, :], ident_d).then_inc(s["const"], 16)
            sp.dma_start(gain[:, :], norm_pre.rearrange("a (k p) -> p (a k)", p=P), allow_slow_non_contiguous=True).then_inc(s["const"], 16)
            for i, g in enumerate((q_gain, k_gain)):
                for h in range(DA_HEADS):
                    sp.dma_start(qk_gain[:, (4 * i + h) * P:(4 * i + h + 1) * P],
                                 g.rearrange("a m d -> a (m d)").broadcast_to([P, P])).then_inc(s["gain_q"], 16)
            for c in range(4):
                sp.dma_start(w[:, :, CUTS[c]:CUTS[c + 1]], w_v[:, :, CUTS[c]:CUTS[c + 1]]).then_inc(s[f"w{c}"], 16)

            def body(b, par, more):
                if more:
                    sp.wait_ge(s["tr_ready"], b * 8 + 4)
                    sp.dma_start(x[:, :, :], x_blocks[b + 1]).then_inc(s["x_loaded"], 16)
                sp.wait_ge(s["cm_evac"], b * NM + NM + 2)
                sp.dma_start(conv_v[b][:, 0:NM - 1, :], conv_out[:, 0:NM - 1, :]).then_inc(s["conv_stored"], 16)
                sp.dma_start(conv_v[b][0:LAST, NM - 1, :], conv_out[0:LAST, NM - 1, :]).then_inc(s["conv_stored"], 16)
                sp.wait_ge(s["tm_act"], b * 10 + 14)
                sp.wait_ge(s["tm_dve"], b * 4 + 8)
                sp.dma_start(v_v[b], tok_out[:, 0, :, :]).then_inc(s["tok_stored"], 16)
                for i in range(2):
                    sp.dma_start(g_v[i][b], tok_out[:, 1 + i, :, :]).then_inc(s["tok_stored"], 16)
                sp.wait_ge(s["tr_evac"], b * 8 + (14 if more else 10))
                sp.sem_inc(s["passed"], 1)
                for i in range(2):
                    sp.dma_start(qk_v[b][i], qk_out[:, i, :, :]).then_inc(s["qk_stored"], 16)

            blocks(sp, body)
            sp.wait_ge(s["conv_stored"], NB * 32 + 32)
            sp.wait_ge(s["tok_stored"], NB * 48 + 48)
            sp.wait_ge(s["qk_stored"], NB * 32 + 32)

        @block.scalar
        def _(act):
            act.sem_inc(s["cm_evac"], 2)
            act.sem_inc(s["tm_act"], 4)
            act.sem_inc(s["conv_stored"], 32)
            act.sem_inc(s["tok_stored"], 48)

            def x_stats(n, first=False):
                act.wait_ge(s["x_loaded"], n * 16 + 16)
                act.wait_ge(s["x_step"], n * 2 + 2)
                if not first:
                    act.wait_ge(s["qk_step"], n * 2)
                for t in range(2):
                    if t:
                        act.wait_ge(s["x_squared"], n * 2 + 1)
                    nc.scalar.activation(junk[:, :], x[:, t, :], ACT.Square, accum_out=xs[:, t, 0:1]).then_inc(s["x_squared"], 1)
                act.wait_ge(s["x_mean"], n + 1)
                nc.scalar.activation(xs[:, :, 1], xs[:, :, 0], ACT.Sqrt).then_inc(s["x_root"], 1)

            def body(b, par, more):
                if more:
                    x_stats(b + 1)
                for m in range(NM):
                    rows = LAST if m == NM - 1 else P
                    act.wait_ge(s["cm_ready"], b * NM + m + 1)
                    if m == 0:
                        act.wait_ge(s["conv_stored"], b * 32 + 32)
                    nc.scalar.copy(conv_out[0:rows, m, :], cm[m % 2][0:rows, 0:BT]).then_inc(s["cm_evac"], 1)
                for t in range(2):
                    for g in range(5):
                        n = 5 * t + g
                        src = tm[(10 * par + n) % 4][:, :]
                        act.wait_ge(s["tm_ready"], b * 10 + n + 1)
                        if g < 2:
                            if g == 0:
                                act.wait_ge(s["tr_ready"], b * 8 + 4 + (0 if t == 0 else (6 if more else 2)))
                            nc.scalar.copy(qk[:, g * 512:g * 512 + 512], src).then_inc(s["tm_act"], 1)
                            if g == 1:
                                act.wait_ge(s["tm_act"], b * 10 + n + 5)
                                act.wait_ge(s["x_squared"], b * 2 + (4 if more else 2))
                                act.wait_ge(s["qk_step"], b * 2 + t + 2)
                                nc.scalar.activation(junk[:, :], qk[:, :], ACT.Square).then_inc(s["qk_squared"], 1)
                                act.wait_ge(s["qk_mean"], b * 2 + t + 1)
                                nc.scalar.activation(qs[:, 1, :], qs[:, 0, :], ACT.Sqrt).then_inc(s["qk_root"], 1)
                        elif g == 2:
                            if t == 0:
                                act.wait_ge(s["tok_stored"], b * 48 + 48)
                            nc.scalar.copy(tok_out[:, 0, t, :], src).then_inc(s["tm_act"], 1)
                        else:
                            nc.scalar.activation(tok_out[:, g - 2, t, :], src, ACT.Tanh, scale=0.5).then_inc(s["tm_act"], 1)

            x_stats(0, True)
            blocks(act, body)

        @block.vector
        def _(dve):
            dve.sem_inc(s["tr_evac"], 2)
            dve.sem_inc(s["tm_dve"], 4)
            dve.sem_inc(s["x_step"], 2)
            dve.sem_inc(s["qk_step"], 2)
            dve.sem_inc(s["qk_stored"], 32)
            dve.wait_ge(s["gain_q"], 8 * 16)
            for h in range(DA_HEADS):
                last = nc.vector.tensor_scalar(qk_gain[:, h * 128:h * 128 + 128], qk_gain[:, h * 128:h * 128 + 128],
                                               DA_DIM ** -0.5 / SLOPES[h], None, ALU.mult)
            last.then_inc(s["gain_q"], 1)
            dve.wait_ge(s["gain_q"], 8 * 16 + 1)

            def x_norm(n):
                dve.wait_ge(s["x_squared"], n * 2 + 2)
                nc.vector.tensor_scalar(xs[:, :, 0], xs[:, :, 0], 1.0 / D_MODEL, NORM_EPS, ALU.mult, ALU.add).then_inc(s["x_mean"], 1)
                dve.wait_ge(s["x_root"], n + 1)
                nc.vector.reciprocal(xs[:, :, 2], xs[:, :, 1]).then_inc(s["x_step"], 1)
                dve.wait_ge(s["x_step"], n * 2 + 3)
                nc.vector.tensor_scalar(x[:, 0, :], x[:, 0, :], xs[:, 0, 2:3], None, ALU.mult).then_inc(s["xn_ready"], 1)
                nc.vector.tensor_scalar(x[:, 1, :], x[:, 1, :], xs[:, 1, 2:3], None, ALU.mult).then_inc(s["xn_ready"], 1)
                dve.wait_ge(s["xn_ready"], n * 2 + 2)
                dve.sem_inc(s["x_step"], 1)

            def x_evac(n, par, base):
                for t in range(2):
                    for hf in range(2):
                        dve.wait_ge(s["tr_ready"], base + 2 * t + hf + 1)
                        nc.vector.tensor_tensor(
                            uT[par][:, 4 * hf:4 * hf + 4, t * P:(t + 1) * P],
                            tr[hf][:, :].rearrange("p (k t) -> p k t", k=4),
                            gain[:, 4 * hf:4 * hf + 4].unsqueeze(2).to_broadcast([P, 4, P]), ALU.mult).then_inc(s["tr_evac"], 1)

            def body(b, par, more):
                if more:
                    x_norm(b + 1)
                    x_evac(b + 1, 1 - par, b * 8 + 4)
                off = 4 if more else 0

                def qk_norm(t):
                    dve.wait_ge(s["qk_squared"], b * 2 + t + 1)
                    nc.vector.tensor_reduce(qs[:, 0, :], junk[:, :].rearrange("p (g d) -> p g d", d=DA_DIM), AX.X, ALU.add).then_inc(s["qk_step"], 1)
                    dve.wait_ge(s["qk_step"], b * 2 + t + 3)
                    nc.vector.tensor_scalar(qs[:, 0, :], qs[:, 0, :], 1.0 / DA_DIM, NORM_EPS, ALU.mult, ALU.add).then_inc(s["qk_mean"], 1)
                    dve.wait_ge(s["qk_root"], b * 2 + t + 1)
                    qk_v3 = qk[:, :].rearrange("p (g d) -> p g d", d=DA_DIM)
                    nc.vector.reciprocal(qs[:, 2, :], qs[:, 1, :]).then_inc(s["qkn_ready"], 1)
                    dve.wait_ge(s["qkn_ready"], b * 6 + t * 3 + 1)
                    nc.vector.tensor_tensor(qk_v3, qk_v3, qs[:, 2, :].unsqueeze(2).to_broadcast([P, 16, DA_DIM]), ALU.mult).then_inc(s["qkn_ready"], 1)
                    dve.wait_ge(s["qkn_ready"], b * 6 + t * 3 + 2)
                    nc.vector.tensor_tensor(qk[:, :], qk[:, :], qk_gain[:, :], ALU.mult).then_inc(s["qkn_ready"], 1)

                def qk_evac(t):
                    for i in range(2):
                        dve.wait_ge(s["tr_ready"], b * 8 + 4 + off + 2 * t + i + 1)
                        if t == 0 and i == 0:
                            dve.wait_ge(s["qk_stored"], b * 32 + 32)
                        nc.vector.tensor_copy(qk_out[:, i, :, t * P:(t + 1) * P],
                                              tr[i][:, :].rearrange("p (h t) -> p h t", h=4)).then_inc(s["tr_evac"], 1)

                def gate(t):
                    for g in (3, 4):
                        n = 5 * t + g
                        dve.wait_ge(s["tm_act"], b * 10 + n + 5)
                        nc.vector.scalar_tensor_tensor(tok_out[:, g - 2, t, :], tok_out[:, g - 2, t, :], 1.0,
                                                       tm[(10 * par + n) % 4][:, :], ALU.add, ALU.mult).then_inc(s["tm_dve"], 1)

                qk_norm(0)
                gate(0)
                qk_evac(0)
                qk_norm(1)
                gate(1)
                qk_evac(1)

            x_norm(0)
            dve.wait_ge(s["const"], 32)
            x_evac(0, 0, 0)
            blocks(dve, body)

        @block.tensor
        def _(pe):
            pe.wait_ge(s["const"], 32)

            def x_transpose(n, base):
                for t in range(2):
                    pe.wait_ge(s["xn_ready"], n * 2 + t + 1)
                    for hf in range(2):
                        pe.wait_ge(s["tr_evac"], base + 2 * t + hf + 1)
                        for k in range(4):
                            c = 4 * hf + k
                            last = nc.tensor.transpose(tr[hf][:, k * P:(k + 1) * P], x[:, t, c * P:(c + 1) * P], ident[:, :])
                        last.then_inc(s["tr_ready"], 1)

            def body(b, par, more):
                u = uT[par]
                off = 4 if more else 0
                pe.wait_ge(s["tr_evac"], b * 8 + 6)
                for m in range(NM):
                    rows = LAST if m == NM - 1 else P
                    if m == 0:
                        pe.wait_ge(s["w0"], 16)
                    if m == 7:
                        pe.wait_ge(s["w1"], 16)
                    pe.wait_ge(s["cm_evac"], b * NM + m + 1)
                    for k in range(KC):
                        last = nc.tensor.matmul(cm[m % 2][0:rows, 0:BT], w[:, k, m * P:m * P + rows], u[:, k, :],
                                                start=(k == 0), stop=(k == KC - 1))
                    last.then_inc(s["cm_ready"], 1)
                if more:
                    x_transpose(b + 1, b * 8 + 4)

                def qk_transpose(t):
                    pe.wait_ge(s["qkn_ready"], b * 6 + t * 3 + 3)
                    for i in range(2):
                        pe.wait_ge(s["tr_evac"], b * 8 + 4 + off + 2 * t + i + 1)
                        for h in range(4):
                            last = nc.tensor.transpose(tr[i][:, h * P:(h + 1) * P], qk[:, (4 * i + h) * P:(4 * i + h + 1) * P], ident[:, :])
                        last.then_inc(s["tr_ready"], 1)

                pe.wait_ge(s["w2"], 16)
                pe.wait_ge(s["w3"], 16)
                for t in range(2):
                    for g in range(5):
                        n = 5 * t + g
                        pe.wait_ge(s["tm_act"], b * 10 + n + 1)
                        if (n - 4) % 5 >= 3:
                            pe.wait_ge(s["tm_dve"], b * 4 + {2: 3, 3: 4, 7: 5, 8: 6}[n])
                        for k in range(KC):
                            last = nc.tensor.matmul(tm[(10 * par + n) % 4][:, :], u[:, k, t * P:(t + 1) * P],
                                                    w[:, k, TOK_COLS[g]:TOK_COLS[g] + 512], start=(k == 0), stop=(k == KC - 1))
                        last.then_inc(s["tm_ready"], 1)
                    if t == 0:
                        qk_transpose(0)
                qk_transpose(1)

            x_transpose(0, 0)
            blocks(pe, body)
T_CONV, T_BIAS, T_W0, T_A0, T_KK, T_KA, T_RK, T_END = 0, 42, 56, 64, 68, 72, 76, 80
PK_F, PK_B, PK_A, PK_BV, PK_R, PK_K, PK_V, PK_END = 0, 129, 258, 386, 514, 642, 770, 898


def vector_table(nc, rows, psum, eng_dma, sem, conv_w, conv_b, w0, a0, k_k, k_a, r_k):
    n = 0

    def load(dst, src):
        nonlocal n
        eng_dma.dma_start(dst, src).then_inc(sem, 16)
        n += 1
    full = CONV_COLS // P
    for i in range(4):
        v = conv_b[0] if i == 3 else conv_w[0, i]
        load(rows[14 * i:14 * i + full, :], v[0:full * P].rearrange("(m p) -> m p", p=P))
        load(rows[14 * i + full:14 * i + full + 1, 0:CONV_COLS - full * P], v[full * P:CONV_COLS].unsqueeze(0))
    load(rows[T_W0:T_W0 + 8, :], w0[0].rearrange("d (g p) -> (d g) p", p=P))
    for at, v in ((T_A0, a0[0]), (T_KK, k_k[0]), (T_KA, k_a[0])):
        load(rows[at:at + 4, :], v.rearrange("(g p) -> g p", p=P))
    load(rows[T_RK:T_RK + 4, :], r_k[0].rearrange("(g h) c -> g (h c)", h=2))
    return n


def prepare_phase(nc, tokens, conv_in, packs, w_up, a_up, ident_d, vectors, table):
    BT = 512
    NB = tokens // BT
    NQ = BT // P
    G = RW_WIDTH // P
    with Phase(nc, "pr") as ph:
        rows = ph.sb("rows", [T_END, P])
        half = ph.sb("half", [P, 12])
        nkk = ph.sb("nkk", [P, 4])
        ka2 = ph.sb("ka2", [P, 2, 4])
        ident = ph.sb("ident", [P, P])
        pair = ph.sb("pair", [P, 2])
        halo = ph.sb("halo", [P, NB, 2])
        zero = ph.sb("zero", [P, 14])
        wup = ph.sb("wup", [P, RW_WIDTH])
        aup = ph.sb("aup", [LORA, RW_WIDTH])
        zwin = ph.sb("zwin", [P, 2, BT + 2])
        zc = ph.sb("zc", [P, 2, BT])
        win = [ph.sb(f"win{i}", [P, 3, BT + 2]) for i in range(2)]
        cc = [ph.sb(f"cc{i}", [P, 3, BT]) for i in range(2)]
        th = [ph.sb(f"th{i}", [P, 3, BT]) for i in range(2)]
        sq = [ph.sb(f"sq{i}", [P, BT]) for i in range(2)]
        pk = [ph.sb(f"pk{i}", [P, NQ, PK_END]) for i in range(2)]
        lw = ph.sb("lw", [P, 2, BT])
        ones = ph.sb("ones", [P, P])
        ua = ph.sb("ua", [P, 2, BT])
        st8 = ph.sb("st8", [P, 3, 8])
        rb = ph.sb("rb", [P, NQ, P])
        lg = [ph.banks(f"lg{i}", 3) for i in range(2)]
        ssb = ph.banks("ss", 1)[0]
        trb = ph.banks("tr", 1)[0]
        s = {n: ph.sem(n) for n in (
            "const", "tab", "rows0", "setup", "pads", "z_loaded", "win0", "win1", "first", "zfirst", "zconv", "tz", "conv_done", "lg_ready", "th_ready",
            "sq_ready", "ss_ready", "var_ready", "root_ready", "rb_ready", "tr_ready", "packed", "stored0", "stored1", "step")}
        block = ph.ctx.enter_context(nc.Block())
        z_v = conv_in[12 * P:14 * P].rearrange("(m p) t -> p m t", p=P)
        c_v = conv_in[0:12 * P].rearrange("(m g p) t -> g p m t", m=3, p=P)
        pk_v = packs[0:G * NB * NQ].rearrange("(g b q) p n -> g b p q n", g=G, q=NQ)

        @block.sync
        def _(sp):
            sp.dma_start(ident[:, :], ident_d).then_inc(s["const"], 16)
            sp.wait_ge(s["rows0"], 2)
            n = vector_table(nc, rows, None, sp, s["tab"], *vectors)
            assert n == 13
            sp.dma_start(wup[:, :], w_up[0].rearrange("d r c -> (d r) c")).then_inc(s["const"], 16)
            sp.dma_start(aup[:, :], a_up[0]).then_inc(s["const"], 16)
            pads = conv_in.rearrange("(m p) t -> p m t", p=P)
            for c in (0, tokens + 1):
                sp.dma_start(pads[:, :, c], zero[:, :], allow_slow_non_contiguous=True).then_inc(s["pads"], 16)
            sp.wait_ge(s["pads"], 32)

            with sp.Fori(1, NB + 1) as after:
                b = after - 1
                sp.wait_ge(s["zconv"], b * 2 + 2)
                sp.dma_start(zwin[:, 0, :], z_v[:, 0, bass.ds(after * BT - BT, BT + 2)]).then_inc(s["z_loaded"], 16)
                sp.dma_start(zwin[0:LORA, 1, :], z_v[0:LORA, 1, bass.ds(after * BT - BT, BT + 2)]).then_inc(s["z_loaded"], 16)
                for g in range(G + 1):
                    if g < G:
                        sp.wait_ge(s["conv_done"], b * 4 + g + 1)
                        sp.dma_start(win[g % 2][:, :, :], c_v[g][:, :, bass.ds(after * BT - BT, BT + 2)]).then_inc(s[f"win{g % 2}"], 16)
                    if g:
                        sp.wait_ge(s["packed"], b * 4 + g + 2)
                        sp.dma_start(pk_v[g - 1][b], pk[(g - 1) % 2][:, :, :]).then_inc(s[f"stored{(g - 1) % 2}"], 16)
            for i in range(2):
                sp.wait_ge(s[f"stored{i}"], NB * 32 + 16)

        @block.gpsimd
        def _(pool):
            nc.gpsimd.memset(rows[:, :], 0.0).then_inc(s["rows0"], 1)
            nc.gpsimd.memset(zero[:, :], 0.0).then_inc(s["rows0"], 1)
            nc.gpsimd.memset(halo[:, :, :], 1.0).then_inc(s["setup"], 1)
            nc.gpsimd.memset(pair[:, :], 0.0).then_inc(s["setup"], 1)
            nc.gpsimd.memset(ones[:, :], 1.0).then_inc(s["setup"], 1)
            for i in range(2):
                nc.gpsimd.memset(pk[i][:, :, PK_F:PK_F + 1], 0.0).then_inc(s["setup"], 1)
                nc.gpsimd.memset(pk[i][:, :, PK_B + P:PK_B + P + 1], 0.0).then_inc(s["setup"], 1)
            pool.wait_ge(s["setup"], 7)
            for n, (dst, value) in enumerate(((halo[:, 0:1, 1:2], 0.0), (halo[:, 1:2, 0:1], 0.0),
                                              (pair[0:64, 0:1], 1.0), (pair[64:128, 1:2], 1.0))):
                nc.gpsimd.memset(dst, value).then_inc(s["setup"], 1)
                pool.wait_ge(s["setup"], 8 + n)

        @block.scalar
        def _(act):
            act.sem_inc(s["tz"], 1)
            act.wait_ge(s["step"], 6)

            def first(g, b, par, slot, src, dst, m):
                rws = LORA if m == 13 else P
                return nc.scalar.activation(dst[0:rws, slot, :], src[0:rws, slot, 1:BT + 1], ACT.Identity,
                                            bias=table[0:rws, T_BIAS + m:T_BIAS + m + 1],
                                            scale=table[0:rws, T_CONV + 14 + m:T_CONV + 14 + m + 1])

            with act.Fori(0, NB) as b:
                act.wait_ge(s["z_loaded"], b * 32 + 32)
                act.wait_ge(s["lg_ready"], b * 4 + 2)
                for i in range(2):
                    first(None, b, 0, i, zwin, zc, 12 + i).then_inc(s["zfirst"], 1)

                def start(g):
                    act.wait_ge(s[f"win{g % 2}"], b * 32 + 16 * (g // 2) + 16)
                    act.wait_ge(s["packed"], b * 4 + g + 1)
                    for i in range(3):
                        first(g, b, g % 2, i, win[g % 2], cc[g % 2], 4 * i + g).then_inc(s["first"], 1)

                def finish(g):
                    i = g % 2
                    act.wait_ge(s["lg_ready"], b * 4 + g + 3)
                    act.wait_ge(s["packed"], b * 4 + g + 1)
                    act.wait_ge(s["th_ready"], b * 12 + 3 * g + 1)
                    for d in range(2):
                        nc.scalar.activation(th[i][:, d, :], lg[i][d][:, :], ACT.Tanh, scale=0.5,
                                             bias=half[:, 4 * d + g:4 * d + g + 1]).then_inc(s["th_ready"], 1)
                    nc.scalar.activation(th[i][:, 2, :], lg[i][2][:, :], ACT.Tanh, scale=0.5,
                                         bias=half[:, 8 + g:9 + g]).then_inc(s["th_ready"], 1)
                    act.wait_ge(s["conv_done"], b * 4 + g + 3)
                    nc.scalar.activation(sq[i][:, :], cc[i][:, 1, :], ACT.Square, scale=nkk[:, g:g + 1]).then_inc(s["sq_ready"], 1)
                    act.wait_ge(s["var_ready"], b * 4 + g + 2)
                    nc.scalar.activation(st8[:, 1, :], st8[:, 0, :], ACT.Sqrt).then_inc(s["root_ready"], 1)

                start(0)
                act.wait_ge(s["zconv"], b * 2 + 4)
                nc.scalar.activation(zc[:, 0, :], zc[:, 0, :], ACT.Tanh).then_inc(s["tz"], 1)
                for g in range(G):
                    if g + 1 < G:
                        start(g + 1)
                    finish(g)

        @block.tensor
        def _(pe):
            pe.sem_inc(s["lg_ready"], 2)
            pe.wait_ge(s["const"], 3 * 16)
            pe.wait_ge(s["tab"], 13 * 16)
            pe.wait_ge(s["setup"], 11)
            nc.tensor.transpose(trb[:, 0:T_END], rows[:, :], ident[0:T_END, 0:T_END]).then_inc(s["tr_ready"], 1)
            with pe.Fori(0, NB) as b:
                for g in range(G):
                    i = g % 2
                    c = slice(g * P, (g + 1) * P)
                    pe.wait_ge(s["tz"], b + 2)
                    pe.wait_ge(s["th_ready"], b * 12 + 3 * g + 3)
                    for d in range(2):
                        nc.tensor.matmul(lg[i][d][:, :], wup[64 * d:64 * d + 64, c], zc[64 * d:64 * d + 64, 0, :], start=True, stop=True)
                    nc.tensor.matmul(lg[i][2][:, :], aup[:, c], zc[0:LORA, 1, :], start=True, stop=True).then_inc(s["lg_ready"], 1)
                    pe.wait_ge(s["sq_ready"], b * 4 + g + 1)
                    pe.wait_ge(s["var_ready"], b * 4 + g + 1)
                    for q in range(NQ):
                        last = nc.tensor.matmul(ssb[:, 2 * q:2 * q + 2], sq[i][:, q * P:(q + 1) * P], pair[:, :], start=True, stop=True)
                    last.then_inc(s["ss_ready"], 1)
                    pe.wait_ge(s["rb_ready"], b * 4 + g + 1)
                    pe.wait_ge(s["packed"], b * 4 + g + 2)
                    for q in range(NQ):
                        last = nc.tensor.transpose(trb[:, q * P:(q + 1) * P], rb[:, q, :], ident[:, :])
                    last.then_inc(s["tr_ready"], 1)

        @block.vector
        def _(dve):
            for n, c in (("zconv", 2), ("conv_done", 2), ("th_ready", 6), ("var_ready", 1), ("packed", 2), ("stored0", 16), ("stored1", 16)):
                dve.sem_inc(s[n], c)
            dve.wait_ge(s["tr_ready"], 1)
            nc.vector.tensor_copy(table[:, :], trb[:, 0:T_END]).then_inc(s["step"], 1)
            dve.wait_ge(s["step"], 1)
            nc.vector.tensor_scalar(half[:, :], table[:, T_W0:T_W0 + 12], 0.5, None, ALU.mult).then_inc(s["step"], 1)
            nc.vector.tensor_scalar(nkk[:, :], table[:, T_KK:T_KK + 4], -1.0, None, ALU.mult).then_inc(s["step"], 1)
            nc.vector.tensor_scalar(ka2[:, 0, :], table[:, T_KA:T_KA + 4], 0.5, None, ALU.mult).then_inc(s["step"], 1)
            nc.vector.tensor_scalar(ka2[:, 1, :], table[:, T_KA:T_KA + 4], -0.5, 1.0, ALU.mult, ALU.add).then_inc(s["step"], 1)
            dve.wait_ge(s["step"], 5)
            dve.wait_ge(s["setup"], 11)
            dve.sem_inc(s["step"], 1)
            PER = 84
            with dve.Fori(0, NB) as b:
                st = Steps(dve, s["step"], b * PER + 6)

                def taps(w_, c_, slot, m, out, rws=P):
                    st.step(nc.vector.scalar_tensor_tensor(c_[0:rws, slot, :], w_[0:rws, slot, 0:BT], table[0:rws, T_CONV + m:T_CONV + m + 1],
                                                           c_[0:rws, slot, :], ALU.mult, ALU.add))
                    st.settle()
                    return nc.vector.scalar_tensor_tensor(out, w_[0:rws, slot, 2:BT + 2], table[0:rws, T_CONV + 28 + m:T_CONV + 29 + m],
                                                          c_[0:rws, slot, :], ALU.mult, ALU.add)

                dve.wait_ge(s["z_loaded"], b * 32 + 32)
                edge = halo[:, bass.ds(b, 1), :]
                st.step(nc.vector.tensor_tensor(zwin[:, 0, 0:BT + 2:BT + 1], zwin[:, 0, 0:BT + 2:BT + 1], edge[:, 0, :], ALU.mult))
                st.step(nc.vector.tensor_tensor(zwin[0:LORA, 1, 0:BT + 2:BT + 1], zwin[0:LORA, 1, 0:BT + 2:BT + 1], edge[0:LORA, 0, :], ALU.mult))
                dve.wait_ge(s["zfirst"], b * 2 + 2)
                st.settle()
                taps(zwin, zc, 0, 12, zc[:, 0, :]).then_inc(s["zconv"], 1)
                taps(zwin, zc, 1, 13, zc[0:LORA, 1, :], LORA).then_inc(s["zconv"], 1)

                def start(g):
                    i = g % 2
                    w_, c_, k_ = win[i], cc[i], pk[i]
                    dve.wait_ge(s[f"win{i}"], b * 32 + 16 * (g // 2) + 16)
                    st.step(nc.vector.tensor_tensor(w_[:, :, 0:BT + 2:BT + 1], w_[:, :, 0:BT + 2:BT + 1],
                                                    edge.broadcast_to([P, 3, 2]), ALU.mult))
                    dve.wait_ge(s["first"], b * 12 + 3 * g + 3)
                    dve.wait_ge(s[f"stored{i}"], b * 32 + 16 * (g // 2) + 16)
                    st.settle()

                    def chunked(at):
                        return k_[:, :, at:at + P]
                    for slot in range(3):
                        st.step(nc.vector.scalar_tensor_tensor(c_[:, slot, :], w_[:, slot, 0:BT], table[:, T_CONV + 4 * slot + g:T_CONV + 4 * slot + g + 1],
                                                               c_[:, slot, :], ALU.mult, ALU.add))
                    st.settle()
                    outs = (chunked(PK_R), c_[:, 1, :].rearrange("p (q t) -> p q t", t=P), chunked(PK_V))
                    for slot in range(3):
                        m = 4 * slot + g
                        ins = nc.vector.scalar_tensor_tensor(outs[slot], w_[:, slot, 2:BT + 2].rearrange("p (q t) -> p q t", t=P),
                                                             table[:, T_CONV + 28 + m:T_CONV + 29 + m],
                                                             c_[:, slot, :].rearrange("p (q t) -> p q t", t=P), ALU.mult, ALU.add)
                        if slot < 2:
                            st.step(ins)
                        else:
                            ins.then_inc(s["conv_done"], 1)

                def finish(g):
                    i = g % 2
                    c_, k_ = cc[i], pk[i]

                    def chunked(at):
                        return k_[:, :, at:at + P]

                    def by_chunk(x):
                        return x.rearrange("p (q t) -> p q t", t=P)
                    dve.wait_ge(s["ss_ready"], b * 4 + g + 1)
                    nc.vector.tensor_scalar(st8[:, 0, :], ssb[:, 0:8], KK_EPS, None, ALU.add).then_inc(s["var_ready"], 1)
                    dve.wait_ge(s["th_ready"], b * 12 + 3 * g + 9)
                    st.step(nc.vector.tensor_scalar(lw[:, :, :], th[i][:, 0:2, :], -W_SCALE / 2, -W_SCALE / 2, ALU.mult, ALU.add))
                    dve.wait_ge(s["packed"], b * 4 + g + 2)
                    st.step(nc.vector.tensor_scalar(ua[:, 0, :], th[i][:, 2, :], ka2[:, 0, g:g + 1], ka2[:, 1, g:g + 1], ALU.mult, ALU.add))
                    st.step(nc.vector.tensor_scalar(ua[:, 1, :], th[i][:, 2, :], -0.5, -0.5, ALU.mult, ALU.add))
                    st.settle()
                    dve.wait_ge(s["root_ready"], b * 4 + g + 1)
                    st.step(nc.vector.reciprocal(st8[:, 2, :], st8[:, 1, :]))
                    for q in range(NQ):
                        lf, lb = lw[:, 0, q * P:(q + 1) * P], lw[:, 1, q * P:(q + 1) * P]
                        st.step(nc.vector.tensor_tensor_scan(k_[:, q, PK_F + 1:PK_F + 1 + P], ones[:, :], lf, 0.0, ALU.mult, ALU.add))
                        if q == 0:
                            dve.wait_ge(s["tr_ready"], b * 4 + g + 1)
                            st.settle()
                            nc.vector.tensor_copy(rb[:, :, :].rearrange("p q (h c) -> p (q h) c", h=2),
                                                  st8[:, 2, :].unsqueeze(2).broadcast_to([P, 8, 64])).then_inc(s["rb_ready"], 1)
                        st.step(nc.vector.tensor_tensor_scan(k_[:, q, PK_B:PK_B + P][:, ::-1], ones[:, :], lb[:, ::-1], 0.0, ALU.mult, ALU.add))
                    st.step(nc.vector.tensor_tensor(chunked(PK_K), by_chunk(c_[:, 1, :]), by_chunk(ua[:, 0, :]), ALU.mult))
                    dve.wait_ge(s["tr_ready"], b * 4 + g + 2)
                    st.step(nc.vector.scalar_tensor_tensor(chunked(PK_A), by_chunk(c_[:, 1, :]), nkk[:, g:g + 1], by_chunk(trb[:, :]), ALU.mult, ALU.mult))
                    st.settle()
                    nc.vector.tensor_tensor(chunked(PK_BV), chunked(PK_A), by_chunk(ua[:, 1, :]), ALU.mult).then_inc(s["packed"], 1)

                start(0)
                for g in range(G):
                    if g + 1 < G:
                        start(g + 1)
                    finish(g)
                assert st.n == PER
def unit_phase(nc, tokens, packs, carry, local, ident_d, table):
    G = RW_WIDTH // P
    NCH = tokens // P
    NI = G * NCH
    with Phase(nc, "un") as ph:
        ident = ph.sb("ident", [P, P])
        ident2 = ph.sb("ident2", [P, 64])
        mask = ph.sb("mask", [P, 2, 4, P])
        pair = ph.sb("pair", [P, 2])
        rk = ph.sb("rk", [P, NI, 2])
        pk = [ph.sb(f"pk{i}", [P, PK_END]) for i in range(2)]
        nm = ph.sb("nm", [P, 2])
        up = ph.sb("up", [P, 2, P + 1])
        down = ph.sb("down", [P, 2, P + 1])
        mid = ph.sb("mid", [P, 2])
        full = ph.sb("full", [P, 2])
        ar = [ph.sb(f"ar{i}", [P, 2, 2, P]) for i in range(2)]
        bk = [ph.sb(f"bk{i}", [P, 2, 2, P]) for i in range(2)]
        aa = [ph.sb(f"aa{i}", [P, 2, P]) for i in range(2)]
        bh = [ph.sb(f"bh{i}", [P, 2, 2, P]) for i in range(2)]
        ad = [ph.sb(f"ad{i}", [P, 2, 256]) for i in range(2)]
        rkk = [ph.sb(f"rkk{i}", [P, P]) for i in range(2)]
        v_tok = ph.sb("v_tok", [P, P])
        ax = ph.sb("ax", [P, 4, P])
        bh_tok = ph.sb("bh_tok", [P, 2, 2, P])
        sm = [ph.sb(f"sm{d}", [P, 2, 4, P]) for d in range(2)]
        a1 = [ph.sb(f"a1{h}", [P, 2, P]) for h in range(2)]
        pw = [[ph.sb(f"pw{d}{k}", [P, 2, 2, P]) for k in range(2)] for d in range(2)]
        tt_ = [[ph.sb(f"tt{d}{k}", [P, 2, P]) for k in range(2)] for d in range(2)]
        wz = [ph.sb(f"wz{d}", [P, 2, P]) for d in range(2)]
        carry_out = [ph.sb(f"carry_out{i}", [P, 2, 256]) for i in range(2)]
        local_out = [ph.sb(f"local_out{i}", [P, 3, P]) for i in range(2)]
        sq = ph.banks("sq", 2)
        tb = ph.banks("tb", 2)
        sc = ph.banks("sc", 2)
        tr = ph.banks("tr", 1)[0]
        ob = ph.banks("ob", 1)[0]
        s = {n: ph.sem(n) for n in (
            "const", "setup", "pk0", "pk1", "exp_ready", "prod", "score_in", "prep_done", "s_ready", "s_evac", "a_evac", "tr_ready",
            "tr_evac", "x_ready", "x_evac", "sq_ready", "sq_evac", "tt_ready", "tt_evac", "wz_ready", "wz_evac", "bonus_ready", "out_ready", "out_evac",
            "y_ready", "y_evac", "carry0", "carry1", "local0", "local1", "rk_ready")}
        block = ph.ctx.enter_context(nc.Block())

        def chunks(eng, body):
            with eng.Fori(0, NI // 2 - 1) as j:
                body(j * 2, j, 0, True)
                body(j * 2 + 1, j, 1, True)
            body(NI - 2, NI // 2 - 1, 0, True)
            body(NI - 1, NI // 2 - 1, 1, False)

        @block.sync
        def _(sp):
            sp.dma_start(ident[:, :], ident_d).then_inc(s["const"], 16)
            for h in range(2):
                sp.dma_start(ident2[64 * h:64 * h + 64, :], ident_d[0:64, 0:64]).then_inc(s["const"], 16)

            def store(n, j, par):
                sp.wait_ge(s["out_evac"], n + 4)
                sp.dma_start(carry[n], carry_out[par][:, :, :]).then_inc(s[f"carry{par}"], 16)
                sp.wait_ge(s["y_evac"], n * 3 + 4)
                sp.dma_start(local[n], local_out[par][:, :, :]).then_inc(s[f"local{par}"], 16)

            for par in range(2):
                sp.dma_start(pk[par][:, :], packs[par]).then_inc(s[f"pk{par}"], 16)
            with sp.Fori(1, NI // 2) as j:
                for par in range(2):
                    n = j * 2 + par
                    store(n - 2, j - 1, par)
                    sp.dma_start(pk[par][:, :], packs[n]).then_inc(s[f"pk{par}"], 16)
            store(NI - 2, NI // 2 - 1, 0)
            store(NI - 1, NI // 2 - 1, 1)
            for par in range(2):
                sp.wait_ge(s[f"carry{par}"], NI * 8 + 16)
                sp.wait_ge(s[f"local{par}"], NI * 8 + 16)

        @block.gpsimd
        def _(pool):
            tt, ts = nc.gpsimd.tensor_tensor, nc.gpsimd.tensor_scalar
            n = 0

            def setup(ins):
                nonlocal n
                n += 1
                ins.then_inc(s["setup"], 1)
                pool.wait_ge(s["setup"], n)
            for d in range(2):
                setup(nc.gpsimd.memset(mask[:, d, :, :], 1.0))
                sign = 1 if d == 0 else -1
                for k in range(4):
                    setup(nc.gpsimd.affine_select(out=mask[:, d, k, :], in_=mask[:, d, k, :], compare_op=ALU.is_gt if k % 2 == 0 else ALU.is_ge,
                                                  fill=0.0, base=0, pattern=[[sign, P]], channel_multiplier=-sign))
                setup(nc.gpsimd.memset(ad[d][:, :, :], 0.0))
            setup(nc.gpsimd.memset(pair[:, :], 0.0))
            for h in range(2):
                setup(nc.gpsimd.memset(pair[64 * h:64 * h + 64, h:h + 1], 1.0))
            assert n == 15
            pool.wait_ge(s["const"], 48)

            def body(n, j, par, more=True):
                p = pk[par]
                st = Steps(pool, s["prod"], n * 14)
                pool.wait_ge(s[f"pk{par}"], j * 16 + 16)
                pool.wait_ge(s["out_evac"], n + 2)
                pool.wait_ge(s["exp_ready"], n * 6 + 6)
                for d in range(2):
                    cur, prev = (1, 0) if d == 0 else (0, 1)
                    st.step(tt(ar[par][:, d, 0, :], p[:, PK_A:PK_A + P], up[:, d, prev:prev + P], ALU.mult))
                    st.step(tt(ar[par][:, d, 1, :], p[:, PK_R:PK_R + P], up[:, d, cur:cur + P], ALU.mult))
                    ins = tt(bk[par][:, d, :, :], p[:, PK_BV:PK_END].rearrange("p (a x) -> p a x", a=2)[:, :, 0:P],
                             down[:, d, cur:cur + P].unsqueeze(1).broadcast_to([P, 2, P]), ALU.mult)
                    if d == 0:
                        st.step(ins)
                    else:
                        ins.then_inc(s["score_in"], 1)
                st.settle()
                pool.wait_ge(s["score_in"], n + 1)
                st.step(tt(rkk[par][:, :], p[:, PK_R:PK_R + P], p[:, PK_K:PK_K + P], ALU.mult))
                for d in range(2):
                    tot = P if d == 0 else 0
                    st.step(ts(aa[par][:, d, :], ar[par][:, d, 0, :], mid[:, d:d + 1], None, ALU.mult))
                    st.step(ts(ad[par][:, d, 64:64 + P], ar[par][:, d, 1, :], mid[:, d:d + 1], None, ALU.mult))
                    st.step(ts(bh[par][:, d, :, :], bk[par][:, d, :, :], up[:, d, tot:tot + 1], None, ALU.mult))
                    st.step(ts(full[:, d:d + 1], mid[:, d:d + 1], up[:, d, tot:tot + 1], None, ALU.mult))
                st.settle()
                for d in range(2):
                    tt(ad[par][:, d, 0:64], ident2[:, :], full[:, d:d + 1].broadcast_to([P, 64]), ALU.mult).then_inc(s["prep_done"], 1)
                assert st.n == 14, st.n

            with pool.Fori(0, NI // 2) as j:
                body(j * 2, j, 0)
                body(j * 2 + 1, j, 1)

        @block.scalar
        def _(act):
            act.sem_inc(s["tr_evac"], 1)

            def exps(n, j, par):
                act.wait_ge(s[f"pk{par}"], j * 16 + 16)
                act.wait_ge(s["prep_done"], n * 2 + 1)
                nc.scalar.mul(nm[:, :], pk[par][:, 64:64 + P + 2:P + 1], -1.0).then_inc(s["exp_ready"], 1)
                act.wait_ge(s["exp_ready"], n * 6 + 1)
                for d in range(2):
                    F = pk[par][:, 129 * d:129 * d + 129]
                    nc.scalar.activation(up[:, d, :], F, ACT.Exp, bias=nm[:, d:d + 1]).then_inc(s["exp_ready"], 1)
                    nc.scalar.activation(down[:, d, :], F, ACT.Exp, scale=-1.0, bias=pk[par][:, 129 * d + 64:129 * d + 65]).then_inc(s["exp_ready"], 1)
                nc.scalar.activation(mid[:, :], nm[:, :], ACT.Exp, scale=-1.0).then_inc(s["exp_ready"], 1)

            def body(n, j, par, more):
                act.wait_ge(s["tr_ready"], n * 2 + 1)
                nc.scalar.copy(v_tok[:, :], tr[:, 0:P]).then_inc(s["tr_evac"], 1)
                nc.scalar.copy(ax[:, :, 0:64], tr[:, P:3 * P].rearrange("p (u c) -> p u c", c=64)).then_inc(s["tr_evac"], 1)
                act.wait_ge(s["tr_ready"], n * 2 + 2)
                nc.scalar.copy(bh_tok[:, :, :, :].rearrange("p d k c -> p (d k c)"), tr[:, :]).then_inc(s["tr_evac"], 1)
                for k in range(1, 7):
                    for d in range(2):
                        act.wait_ge(s["sq_ready"], n * 12 + 2 * (k - 1) + d + 1)
                        nc.scalar.copy(pw[d][k % 2][:, :, :, :].rearrange("p u a c -> p (u a c)"), sq[d][:, :]).then_inc(s["sq_evac"], 1)
                    if k == 2 and more:
                        exps(n + 1, j + par, 1 - par)
                for d in range(2):
                    act.wait_ge(s["wz_ready"], n * 2 + d + 1)
                    nc.scalar.copy(wz[d][:, :, :].rearrange("p u c -> p (u c)"), sq[d][:, 0:256]).then_inc(s["wz_evac"], 1)

            exps(0, 0, 0)
            chunks(act, body)

        @block.vector
        def _(dve):
            for n, c in (("s_evac", 2), ("out_evac", 3), ("y_evac", 1), ("prep_done", 1), ("carry0", 16), ("carry1", 16), ("local0", 16), ("local1", 16)):
                dve.sem_inc(s[n], c)
            dve.wait_ge(s["setup"], 15)
            dve.wait_ge(s["const"], 48)
            for g in range(G):
                last = nc.vector.tensor_scalar(rk[:, g * NCH:(g + 1) * NCH, :], pair[:, :].unsqueeze(1).broadcast_to([P, NCH, 2]),
                                               table[:, T_RK + g:T_RK + g + 1], None, ALU.mult)
            last.then_inc(s["rk_ready"], 1)

            def body(n, j, par, more):
                for d in range(2):
                    for h in range(2):
                        u = 2 * d + h
                        dve.wait_ge(s["s_ready"], n * 4 + u + 1)
                        nc.vector.tensor_tensor(sm[d][:, h, :, :], sc[h][:, :].rearrange("p (k t) -> p k t", k=4), mask[:, d, :, :], ALU.mult).then_inc(s["s_evac"], 1)
                    dve.wait_ge(s["s_evac"], n * 4 + 2 * d + 4)
                    nc.vector.tensor_tensor(tt_[d][1][:, :, :], sm[d][:, :, 0, :], ident[:, :].unsqueeze(1).broadcast_to([P, 2, P]), ALU.add).then_inc(s["tt_evac"], 1)
                for h in range(2):
                    nc.vector.tensor_tensor(a1[h][:, :, :], tb[h][:, 256:512].rearrange("p (d t) -> p d t", d=2),
                                            mask[:, ::-1, 0, :], ALU.mult).then_inc(s["a_evac"], 1)
                for d in range(2):
                    dve.wait_ge(s["x_ready"], n * 2 + d + 1)
                    nc.vector.tensor_copy(ax[:, 2 * d:2 * d + 2, 64:128], tb[d][:, 0:128].rearrange("p (h c) -> p h c", h=2)).then_inc(s["x_evac"], 1)
                for k in range(2, 8):
                    for d in range(2):
                        dve.wait_ge(s["tt_ready"], n * 12 + 2 * (k - 2) + d + 1)
                        dve.wait_ge(s["tt_evac"], n * 14 + 2 * (k - 2) + d + 1)
                        nc.vector.tensor_tensor(tt_[d][k % 2][:, :, :], tt_[d][(k - 1) % 2][:, :, :],
                                                tb[d][:, 0:256].rearrange("p (h t) -> p h t", h=2), ALU.add).then_inc(s["tt_evac"], 1)
                dve.wait_ge(s[f"carry{par}"], j * 16 + 16)
                dve.wait_ge(s["prep_done"], n * 2 + 3)
                dve.wait_ge(s["out_ready"], n + 1)
                nc.vector.tensor_tensor(carry_out[par][:, :, :], ob[:, :].rearrange("p (d c) -> p d c", d=2), ad[par][:, :, :], ALU.add).then_inc(s["out_evac"], 1)
                dve.wait_ge(s[f"local{par}"], j * 16 + 16)
                dve.wait_ge(s["y_ready"], n + 1)
                nc.vector.tensor_copy(local_out[par][:, 0:2, :].rearrange("p d c -> p (d c)"), sc[0][:, 0:256]).then_inc(s["y_evac"], 1)
                for h in range(2):
                    nc.vector.tensor_scalar(local_out[par][:, 2, 64 * h:64 * h + 64], v_tok[:, 64 * h:64 * h + 64], sc[1][:, h:h + 1], None, ALU.mult).then_inc(s["y_evac"], 1)

            chunks(dve, body)

        @block.tensor
        def _(pe):
            pe.wait_ge(s["const"], 48)
            pe.wait_ge(s["rk_ready"], 1)
            mm = nc.tensor.matmul

            def body(n, j, par, more):
                A, B = ar[par], bk[par]
                pe.wait_ge(s["score_in"], n + 1)
                pe.wait_ge(s["y_evac"], n * 3 + 1)
                for u in range(4):
                    d, h = u // 2, u % 2
                    hs = slice(64 * h, 64 * h + 64)
                    pe.wait_ge(s["s_evac"], n * 4 + u + 1)
                    rhs = A[hs, d, :, :].rearrange("p k t -> p (k t)")
                    mm(sc[h][:, 0:256], B[hs, d, 0, :], rhs, start=True, stop=True)
                    mm(sc[h][:, 256:512], B[hs, d, 1, :], rhs, start=True, stop=True)
                    mm(tb[h][:, 256 + P * d:384 + P * d], A[hs, d, 0, :], B[hs, d, 0, :], start=True, stop=True).then_inc(s["s_ready"], 1)
                pe.wait_ge(s["prep_done"], n * 2 + 3)
                pe.wait_ge(s["tr_evac"], n * 3 + 1)
                for k, src in enumerate((pk[par][:, PK_V:PK_V + P], aa[par][:, 0, :], aa[par][:, 1, :])):
                    last = nc.tensor.transpose(tr[:, k * P:(k + 1) * P], src, ident[:, :])
                last.then_inc(s["tr_ready"], 1)
                for d in range(2):
                    pe.wait_ge(s["a_evac"], n * 2 + 2)
                    for h in range(2):
                        AT, A1 = sm[d][:, h, 0, :], a1[h][:, d, :]
                        mm(sq[d][:, 256 * h:256 * h + P], AT, A1, start=True, stop=True)
                        last = mm(sq[d][:, 256 * h + P:256 * h + 256], A1, AT, start=True, stop=True)
                    last.then_inc(s["sq_ready"], 1)
                    if d == 0:
                        pe.wait_ge(s["tr_evac"], n * 3 + 3)
                        for k in range(4):
                            last = nc.tensor.transpose(tr[:, k * P:(k + 1) * P], bh[par][:, k // 2, k % 2, :], ident[:, :])
                        last.then_inc(s["tr_ready"], 1)
                    for h in range(2):
                        last = mm(tb[d][:, 64 * h:64 * h + 64], sm[d][:, h, 2, :], v_tok[:, 64 * h:64 * h + 64], start=True, stop=True)
                    last.then_inc(s["x_ready"], 1)
                for k in range(2, 8):
                    for d in range(2):
                        w, t = pw[d][(k - 1) % 2], tt_[d][(k - 1) % 2]
                        pe.wait_ge(s["sq_evac"], n * 12 + 2 * (k - 2) + d + 1)
                        if k < 7:
                            for h in range(2):
                                last = mm(sq[d][:, 256 * h:256 * h + P], w[:, h, 1, :], w[:, h, 0, :], start=True, stop=True)
                                if k < 6:
                                    last = mm(sq[d][:, 256 * h + P:256 * h + 256], w[:, h, 0, :], w[:, h, 1, :], start=True, stop=True)
                            last.then_inc(s["sq_ready"], 1)
                        pe.wait_ge(s["tt_evac"], n * 14 + 2 * (k - 2) + d + 1)
                        if k == 2:
                            pe.wait_ge(s["x_evac"], n * 2 + d + 1)
                        for h in range(2):
                            last = mm(tb[d][:, P * h:P * h + P], w[:, h, 0, :], t[:, h, :], start=True, stop=True)
                        last.then_inc(s["tt_ready"], 1)
                mm(sc[1][:, 0:2], rkk[par][:, :], rk[:, bass.ds(n, 1), :].rearrange("p a c -> p (a c)"), start=True, stop=True)
                for d in range(2):
                    pe.wait_ge(s["tt_evac"], n * 14 + 12 + d + 1)
                    for h in range(2):
                        last = mm(sq[d][:, P * h:P * h + P], tt_[d][1][:, h, :], ax[:, 2 * d + h, :], start=True, stop=True)
                    last.then_inc(s["wz_ready"], 1)
                pe.wait_ge(s["out_evac"], n + 3)
                for u in range(4):
                    d, h = u // 2, u % 2
                    hs = slice(64 * h, 64 * h + 64)
                    W, Z = wz[d][:, h, 0:64], wz[d][:, h, 64:128]
                    o = ob[hs, 256 * d:256 * d + 256]
                    pe.wait_ge(s["wz_evac"], n * 2 + d + 1)
                    mm(o[:, 0:64], W, bh_tok[:, d, 0, hs], start=True, stop=True)
                    mm(o[:, 64:192], W, sm[d][:, h, 1, :], start=True, stop=True)
                    mm(o[:, 192:256], bh_tok[:, d, 0, hs], Z, start=True, stop=False)
                    last = mm(o[:, 192:256], bh_tok[:, d, 1, hs], v_tok[:, hs], start=False, stop=True)
                    if u == 3:
                        last.then_inc(s["out_ready"], 1)
                for u in range(4):
                    d, h = u // 2, u % 2
                    hs = slice(64 * h, 64 * h + 64)
                    mm(sc[0][:, 64 * u:64 * u + 64], sm[d][:, h, 1, :], wz[d][:, h, 64:128], start=True, stop=False)
                    last = mm(sc[0][:, 64 * u:64 * u + 64], sm[d][:, h, 3, :], v_tok[:, hs], start=False, stop=True)
                last.then_inc(s["y_ready"], 1)

            chunks(pe, body)
def chain_phase(nc, tokens, sequences, carry, local, y):
    G = RW_WIDTH // P
    NCH = tokens // P
    with Phase(nc, "ch") as ph:
        cb = [ph.sb(f"cb{i}", [P, 2, G, 256]) for i in range(2)]
        lb = [ph.sb(f"lb{i}", [P, 2, G, P]) for i in range(2)]
        yo = [ph.sb(f"yo{i}", [P, 2, G, P]) for i in range(2)]
        H = [ph.sb(f"H{i}", [P, 2 * G, 64]) for i in range(2)]
        hb = ph.banks("hb", 2)
        yb = ph.banks("yb", 4)
        s = {n: ph.sem(n) for n in ("loaded0", "loaded1", "h_ready", "h_evac", "y_ready", "y_evac", "stored0", "stored1", "passed")}
        block = ph.ctx.enter_context(nc.Block())
        carry_v = carry.rearrange("(g c) p d n -> c d p g n", g=G)
        local_v = local.rearrange("(g c) p k n -> c k p g n", g=G)
        y_v = y.rearrange("d (c p) n -> d c p n", p=P)

        def steps(eng, body, start=None):
            for i, (first, count) in enumerate(sequences):
                if start:
                    start(i, first)
                with eng.Fori(0, count // 2) as j:
                    for par in range(2):
                        t = j * 2 + (first + par)
                        body(t, (t, j * -2 + (first + count - 1 - par)), par, j + first // 2, i)

        @block.sync
        def _(sp):
            def body(t, chunk, par, half, i):
                sp.wait_ge(s["y_evac"], t * 4 + 1)
                for d in range(2):
                    sp.dma_start(cb[par][:, d, :, :], carry_v[chunk[d]][d]).then_inc(s[f"loaded{par}"], 16)
                    sp.dma_start(lb[par][:, d, :, :], local_v[chunk[d]][d]).then_inc(s[f"loaded{par}"], 16)
            steps(sp, body)

        @block.scalar
        def _(act):
            def body(t, chunk, par, half, i):
                act.wait_ge(s["y_evac"], t * 4 + 9)
                for d in range(2):
                    act.dma_start(y_v[d][chunk[d]], yo[par][:, d, :, :].rearrange("p g c -> p (g c)")).then_inc(s[f"stored{par}"], 16)
            steps(act, body)
            for par in range(2):
                act.wait_ge(s[f"stored{par}"], NCH * 16 + 32)

        @block.vector
        def _(dve):
            dve.sem_inc(s["y_evac"], 5)
            for par in range(2):
                dve.sem_inc(s[f"stored{par}"], 32)

            def start(i, first):
                if i:
                    dve.wait_ge(s["h_evac"], first + i)
                nc.vector.memset(H[0][:, :, :], 0.0).then_inc(s["h_evac"], 1)

            def body(t, chunk, par, half, i):
                dve.wait_ge(s["h_ready"], t + 1)
                nc.vector.tensor_tensor(H[1 - par][:, :, :], hb[par][:, :].rearrange("p (u c) -> p u c", c=64),
                                        cb[par][:, :, :, 192:256].rearrange("p d g c -> p (d g) c"), ALU.add).then_inc(s["h_evac"], 1)
                dve.wait_ge(s["stored%d" % par], half * 32 + 32)
                dve.wait_ge(s["y_ready"], t + 1)
                for d in range(2):
                    for h in range(2):
                        nc.vector.tensor_tensor(yo[par][:, d, :, 64 * h:64 * h + 64], yb[2 * d + h][:, 0:256].rearrange("p (g c) -> p g c", c=64),
                                                lb[par][:, d, :, 64 * h:64 * h + 64], ALU.add).then_inc(s["y_evac"], 1)
            steps(dve, body, start)

        @block.tensor
        def _(pe):
            def body(t, chunk, par, half, i):
                pe.wait_ge(s[f"loaded{par}"], half * 64 + 64)
                pe.wait_ge(s["h_evac"], t + i + 1)
                pe.sem_inc(s["passed"], 1)
                units = [(d, g, h) for h in range(2) for d in range(2) for g in range(G)]
                for d, g, h in units:
                    hs = slice(64 * h, 64 * h + 64)
                    u = G * d + g
                    last = nc.tensor.matmul(hb[par][hs, 64 * u:64 * u + 64], cb[par][hs, d, g, 0:64], H[par][hs, u, :], start=True, stop=True)
                last.then_inc(s["h_ready"], 1)
                pe.wait_ge(s["y_evac"], t * 4 + 5)
                for d, g, h in units:
                    hs = slice(64 * h, 64 * h + 64)
                    last = nc.tensor.matmul(yb[2 * d + h][:, 64 * g:64 * g + 64], cb[par][hs, d, g, 64:192], H[par][hs, G * d + g, :], start=True, stop=True)
                last.then_inc(s["y_ready"], 1)
            steps(pe, body)


def attention_phase(nc, name, first, count, q_kT, v_tok, o_tok, lam_d, ident_d):
    S = count * P
    NB = S // 512
    W = min(S, 1024)
    NG = S // W
    GP = 2 * NG
    t0 = first * P
    HD = DA_HEADS
    with Phase(nc, name) as ph:
        kT = ph.sb("kT", [P, HD, S])
        v = ph.sb("v", [P, count, DA_WIDTH])
        qz = [ph.sb(f"qz{i}", [P, HD, 2, P]) for i in range(2)]
        wide = ph.sb("wide", [P, 2 * S - P])
        nd = [ph.sb(f"nd{i}", [P, S]) for i in range(2)]
        sc = [[ph.sb(f"sc{i}{m}", [P, S]) for m in range(2)] for i in range(2)]
        attT = [ph.sb(f"attT{i}", [P, count, P]) for i in range(2)]
        o = [ph.sb(f"o{i}", [P, DA_WIDTH]) for i in range(2)]
        mx = ph.sb("mx", [P, 2, 2, 2])
        nm = ph.sb("nm", [P, 2, 2])
        rs = ph.sb("rs", [P, 2, 2])
        ri = ph.sb("ri", [P, 2, 2])
        cf = ph.sb("cf", [P, 2])
        ident = ph.sb("ident", [P, P])
        lv = ph.sb("lv", [P, 4, DA_DIM])
        lp = ph.sb("lp", [P, 2, DA_DIM])
        ls = ph.sb("ls", [P, 4])
        nlam = ph.sb("nlam", [P, 1])
        gb = [ph.ctx.enter_context(nc.psum_tensor(f"{name}_g{i}", [P, W], F32)) for i in range(2)]
        tb = ph.banks("tb", 2)
        pb = ph.banks("pb", 2)
        s = {n: ph.sem(n) for n in (
            "const", "kv", "lam", "lam_exp", "wide0", "wide1", "zero", "q0", "q1", "sc_ready", "red", "nm_ready", "exp_done", "att_step", "att_done",
            "tp_ready", "tp_evac", "pv_ready", "pv_evac", "nd_ready", "stored0", "stored1", "passed")}
        block = ph.ctx.enter_context(nc.Block())
        q_v = q_kT[0:DA_WIDTH, t0:t0 + S].rearrange("(h m d) (c t) -> c m d h t", h=HD, m=2, t=P)
        k_v = q_kT[DA_WIDTH:2 * DA_WIDTH, t0:t0 + S].rearrange("(h r) t -> r h t", r=P)
        v_v = v_tok[t0:t0 + S].rearrange("(c p) n -> p c n", p=P)
        o_v = o_tok[t0:t0 + S].rearrange("(c p) n -> c p n", p=P)

        def tiles(eng, body):
            if count > 2:
                with eng.Fori(0, count // 2 - 1) as j:
                    body(j * 2, j, 0, True)
                    body(j * 2 + 1, j, 1, True)
            body(count - 2, count // 2 - 1, 0, True)
            body(count - 1, count // 2 - 1, 1, False)

        @block.sync
        def _(sp):
            sp.dma_start(ident[:, :], ident_d).then_inc(s["const"], 16)
            sp.dma_start(lv[:, :, :].rearrange("p a d -> p (a d)"), lam_d.rearrange("o a d -> o (a d)").broadcast_to([P, 4 * DA_DIM])).then_inc(s["const"], 16)

            def load_q(n, par):
                for m in range(2):
                    sp.dma_start(qz[par][64 * m:64 * m + 64, :, m, :], q_v[n][m]).then_inc(s[f"q{par}"], 16)
            sp.wait_ge(s["zero"], 2)
            load_q(0, 0)
            sp.dma_start(kT[:, :, :], k_v).then_inc(s["kv"], 16)
            sp.dma_start(v[:, :, :], v_v).then_inc(s["kv"], 16)
            load_q(1, 1)

            def body(n, j, par, more):
                if more and not (isinstance(n, int) and n + 2 >= count):
                    sp.wait_ge(s["sc_ready"], n * (4 * GP) + 4 * GP)
                    load_q(n + 2, par)
                sp.wait_ge(s["pv_evac"], n * 4 + 6)
                sp.dma_start(o_v[n], o[par][:, :]).then_inc(s[f"stored{par}"], 16)
            tiles(sp, body)
            for par in range(2):
                sp.wait_ge(s[f"stored{par}"], count * 8 + 16)

        @block.gpsimd
        def _(pool):
            for i in range(2):
                nc.gpsimd.memset(qz[i][:, :, :, :], 0.0).then_inc(s["zero"], 1)
            nc.gpsimd.iota(wide[:, :], pattern=[[-1, 2 * S - P]], base=S - P, channel_multiplier=1,
                           allow_small_or_imprecise_dtypes=True).then_inc(s["wide0"], 1)

        @block.scalar
        def _(act):
            act.sem_inc(s["tp_evac"], 2)
            act.sem_inc(s["pv_evac"], 2)
            for i in range(2):
                act.sem_inc(s[f"stored{i}"], 16)
            act.wait_ge(s["lam"], 3)
            nc.scalar.activation(ls[:, 2:4], ls[:, 0:2], ACT.Exp).then_inc(s["lam_exp"], 1)

            def distances(n, par):
                nc.scalar.copy(nd[par][:, :], wide[:, bass.ds(n * -P + (count - 1) * P, S)]).then_inc(s["nd_ready"], 1)

            def exp(n, h, m):
                act.wait_ge(s["nm_ready"], n * 8 + 2 * h + m + 1)
                nc.scalar.activation(sc[h % 2][m][:, :], sc[h % 2][m][:, :], ACT.Exp, bias=nm[:, h % 2, m:m + 1],
                                     accum_out=rs[:, h % 2, m:m + 1]).then_inc(s["exp_done"], 1)

            act.wait_ge(s["wide1"], 1)
            distances(0, 0)
            exp(0, 0, 0)
            exp(0, 0, 1)

            def body(n, j, par, more):
                for h in range(HD):
                    nxt = (n, h + 1) if h + 1 < HD else ((n + 1, 0) if more else None)
                    if nxt:
                        exp(*nxt, 0)
                    act.wait_ge(s["pv_ready"], n * 4 + h + 1)
                    for k in range(NB):
                        i = NB * h + k
                        act.wait_ge(s["tp_ready"], n * (4 * NB) + i + 2 + NB)
                        nc.scalar.copy(attT[h % 2][:, 4 * k:4 * k + 4, :].rearrange("p c q -> p (c q)"), tb[(k if NB > 1 else h) % 2][:, :]).then_inc(s["tp_evac"], 1)
                    if nxt:
                        exp(*nxt, 1)
                    act.wait_ge(s["pv_ready"], n * 4 + h + 3)
                    if h == 0:
                        act.wait_ge(s[f"stored{par}"], j * 16 + 16)
                    nc.scalar.activation(o[par][:, h * P:(h + 1) * P], pb[h % 2][:, 0:P], ACT.Copy, scale=ri[:, h % 2, 0:1]).then_inc(s["pv_evac"], 1)
                    if h == 1 and more:
                        distances(n + 1, 1 - par)
            tiles(act, body)

        @block.vector
        def _(dve):
            dve.sem_inc(s["red"], 2)
            dve.wait_ge(s["const"], 32)
            nc.vector.tensor_tensor(lp[:, :, :], lv[:, 0:4:2, :], lv[:, 1:4:2, :], ALU.mult).then_inc(s["lam"], 1)
            dve.wait_ge(s["lam"], 1)
            nc.vector.tensor_reduce(ls[:, 0:2], lp[:, :, :], AX.X, ALU.add).then_inc(s["lam"], 1)
            dve.wait_ge(s["wide0"], 1)
            nc.vector.scalar_tensor_tensor(wide[:, :], wide[:, :], -1.0, wide[:, :], ALU.mult, ALU.min).then_inc(s["wide1"], 1)
            dve.wait_ge(s["lam"], 2)
            dve.sem_inc(s["lam"], 1)
            dve.wait_ge(s["lam_exp"], 1)
            nc.vector.tensor_tensor(nlam[:, :], ls[:, 3:4], ls[:, 2:3], ALU.subtract).then_inc(s["lam"], 1)
            dve.wait_ge(s["lam"], 4)
            nc.vector.tensor_scalar(nlam[:, :], nlam[:, :], -LAM_INIT, None, ALU.add).then_inc(s["lam"], 1)
            dve.wait_ge(s["lam"], 5)

            def reduce(n, par, h, m):
                i = h % 2
                if m == 0:
                    dve.wait_ge(s["nd_ready"], n + 1)
                    dve.wait_ge(s["tp_ready"], n * (4 * NB) + NB * h + 1)
                for k in range(NG):
                    g = m * NG + k
                    dve.wait_ge(s["sc_ready"], n * (4 * GP) + GP * h + g + 1)
                    dve.sem_inc(s["passed"], 1)
                    nc.vector.tensor_tensor_reduce(out=sc[i][m][:, k * W:(k + 1) * W], in0=gb[g % 2][:, :], in1=nd[par][:, k * W:(k + 1) * W],
                                                   scale=SLOPES[h], scalar=-3e38, op0=ALU.add, op1=ALU.max,
                                                   accum_out=mx[:, i, m, k:k + 1]).then_inc(s["red"], 1)
                dve.wait_ge(s["red"], n * (4 * GP) + GP * h + (m + 1) * NG + 2)
                nc.vector.tensor_scalar(nm[:, i, m:m + 1], mx[:, i, m, 0:1], mx[:, i, m, NG - 1:NG], -1.0, ALU.max, ALU.mult).then_inc(s["nm_ready"], 1)

            def combine(n, h):
                i = h % 2
                dve.wait_ge(s["exp_done"], n * 8 + 2 * h + 2)
                nc.vector.reciprocal(ri[:, i, :], rs[:, i, :]).then_inc(s["att_step"], 1)
                dve.wait_ge(s["att_step"], n * 8 + 2 * h + 1)
                nc.vector.scalar_tensor_tensor(cf[:, i:i + 1], rs[:, i, 0:1], ri[:, i, 1:2], nlam[:, :], ALU.mult, ALU.mult).then_inc(s["att_step"], 1)
                dve.wait_ge(s["att_step"], n * 8 + 2 * h + 2)
                nc.vector.scalar_tensor_tensor(sc[i][0][:, :], sc[i][1][:, :], cf[:, i:i + 1], sc[i][0][:, :], ALU.mult, ALU.add).then_inc(s["att_done"], 1)

            reduce(0, 0, 0, 0)
            reduce(0, 0, 0, 1)

            def body(n, j, par, more):
                for h in range(HD):
                    nxt = (n, par, h + 1) if h + 1 < HD else ((n + 1, 1 - par, 0) if more else None)
                    if nxt:
                        reduce(*nxt, 0)
                    combine(n, h)
                    if nxt:
                        reduce(*nxt, 1)
            tiles(dve, body)

        @block.tensor
        def _(pe):
            pe.sem_inc(s["tp_ready"], NB + 1)
            pe.sem_inc(s["pv_ready"], 2)
            pe.wait_ge(s["const"], 32)
            pe.wait_ge(s["kv"], 32)

            def scores(n, j, par, h):
                if h == 0:
                    pe.wait_ge(s[f"q{par}"], j * 32 + 32)
                for m in range(2):
                    for k in range(NG):
                        g = m * NG + k
                        pe.wait_ge(s["red"], n * (4 * GP) + GP * h + g + 1)
                        for c in range(W // 512):
                            at = k * W + c * 512
                            last = nc.tensor.matmul(gb[g % 2][:, c * 512:(c + 1) * 512], qz[par][:, h, m, :], kT[:, h, at:at + 512], start=True, stop=True)
                        last.then_inc(s["sc_ready"], 1)

            scores(0, 0, 0, 0)

            def body(n, j, par, more):
                for h in range(HD):
                    if h + 1 < HD:
                        scores(n, j, par, h + 1)
                    elif more:
                        scores(n + 1, j + par, 1 - par, 0)
                    pe.wait_ge(s["att_done"], n * 4 + h + 1)
                    for k in range(NB):
                        pe.wait_ge(s["tp_evac"], n * (4 * NB) + NB * h + k + 1)
                        for c in range(4):
                            last = nc.tensor.transpose(tb[(k if NB > 1 else h) % 2][:, c * P:(c + 1) * P], sc[h % 2][0][:, (4 * k + c) * P:(4 * k + c + 1) * P], ident[:, :])
                        last.then_inc(s["tp_ready"], 1)
                    pe.wait_ge(s["tp_evac"], n * (4 * NB) + NB * h + NB + 2)
                    pe.wait_ge(s["pv_evac"], n * 4 + h + 1)
                    for c in range(count):
                        last = nc.tensor.matmul(pb[h % 2][:, 0:P], attT[h % 2][:, c, :], v[:, c, h * P:(h + 1) * P], start=(c == 0), stop=(c == count - 1))
                    last.then_inc(s["pv_ready"], 1)
            tiles(pe, body)
def output_phase(nc, tokens, x_t, p_t, y, local, gates, o_tok, out_t, w_out, ple_proj, gate_w, rows, ident_d):
    G = RW_WIDTH // P
    NT = tokens // P
    HALF = D_MODEL // 2
    ln_g_d, ln_b_d, subln_d, ple_norm_d, gate_b_d = rows
    with Phase(nc, "fn") as ph:
        wo = ph.sb("wo", [P, KC, D_MODEL])
        wg = ph.sb("wg", [P, KC, D_MODEL])
        wp = ph.sb("wp", [P, 2, D_MODEL])
        ident = ph.sb("ident", [P, P])
        ln_g, ln_b, subln = ph.sb("ln_g", [P, 512]), ph.sb("ln_b", [P, 512]), ph.sb("subln", [P, 512])
        ple_norm, gate_b = ph.sb("ple_norm", [P, D_MODEL]), ph.sb("gate_b", [P, D_MODEL])
        x = [ph.sb(f"x{i}", [P, D_MODEL]) for i in range(2)]
        p = [ph.sb(f"p{i}", [P, D_PLE]) for i in range(2)]
        yb = [ph.sb(f"yb{i}", [P, 2, 512]) for i in range(2)]
        bonus = [ph.sb(f"bonus{i}", [P, G, P]) for i in range(2)]
        gt = [ph.sb(f"gt{i}", [P, 2, 512]) for i in range(2)]
        o = [ph.sb(f"o{i}", [P, 512]) for i in range(2)]
        yy = ph.sb("yy", [P, 512])
        junk = ph.sb("junk", [P, 2, 512])
        st12 = ph.sb("st12", [P, 4, 12])
        mix = ph.sb("mix", [P, D_MODEL])
        mixT, hT, pT = ph.sb("mixT", [P, KC, P]), ph.sb("hT", [P, KC, P]), ph.sb("pT", [P, 2, P])
        h = ph.sb("h", [P, D_MODEL])
        es = ph.sb("es", [P, 5])
        ejunk = ph.sb("ejunk", [P, 512])
        en = ph.sb("en", [P, D_MODEL])
        zz = ph.sb("zz", [P, D_MODEL])
        out = [ph.sb(f"out{i}", [P, D_MODEL]) for i in range(2)]
        tr = ph.banks("tr", 2)
        hb = ph.banks("hb", 2)
        eb = ph.banks("eb", 2)
        gb = ph.banks("gb", 2)
        s = {n: ph.sem(n) for n in (
            "ident", "wo", "wp", "wg", "rows", "scaled", "in0", "in1", "centred", "sq_done", "var", "root", "mixed", "tr_ready", "tr_evac", "h_mm", "h_ready",
            "e_mm", "e_sq", "e_var", "e_root", "en_done", "g_mm", "z_ready", "th_ready", "out_ready", "stored0", "stored1", "step", "tail")}
        block = ph.ctx.enter_context(nc.Block())
        bonus_v = local.rearrange("(g c) p k n -> c k p g n", g=G)
        y_v = y.rearrange("d (c p) n -> c p d n", p=P)
        g_v = [g.rearrange("(c p) n -> c p n", p=P) for g in gates]
        o_v = o_tok.rearrange("(c p) n -> c p n", p=P)
        w_v = [w.rearrange("(k p) n -> p k n", p=P) for w in (w_out, gate_w, ple_proj)]

        def tiles(eng, body):
            with eng.Fori(0, NT // 2 - 1) as j:
                body(j * 2, j, 0, True)
                body(j * 2 + 1, j, 1, True)
            body(NT - 2, NT // 2 - 1, 0, True)
            body(NT - 1, NT // 2 - 1, 1, False)

        @block.sync
        def _(sp):
            def load(n, par):
                for dst, src in ((yb[par][:, :, :], y_v[n]), (o[par][:, :], o_v[n]), (bonus[par][:, :, :], bonus_v[n][2]),
                                 (gt[par][:, 0, :], g_v[0][n]), (gt[par][:, 1, :], g_v[1][n]), (x[par][:, :], x_t[n]), (p[par][:, :], p_t[n])):
                    sp.dma_start(dst, src).then_inc(s[f"in{par}"], 16)
            load(0, 0)
            sp.dma_start(ident[:, :], ident_d).then_inc(s["ident"], 16)
            sp.dma_start(subln[:, 0:P], subln_d.broadcast_to([P, P])).then_inc(s["rows"], 16)
            for dst, src, n in ((ln_g, ln_g_d, 512), (ln_b, ln_b_d, 512), (ple_norm, ple_norm_d, D_MODEL), (gate_b, gate_b_d, D_MODEL)):
                sp.dma_start(dst[:, :], src.broadcast_to([P, n])).then_inc(s["rows"], 16)
            sp.dma_start(wo[:, :, :], w_v[0]).then_inc(s["wo"], 16)
            sp.dma_start(wp[:, :, :], w_v[2]).then_inc(s["wp"], 16)
            sp.dma_start(wg[:, :, :], w_v[1]).then_inc(s["wg"], 16)
            load(1, 1)

            def body(n, j, par, more):
                if more and not (isinstance(n, int) and n + 2 >= NT):
                    sp.wait_ge(s["h_ready"], n * 2 + 2)
                    sp.wait_ge(s["tr_ready"], n * 5 + 3)
                    load(n + 2, par)
                sp.wait_ge(s["out_ready"], n + 1)
                sp.dma_start(out_t[n], out[par][:, :]).then_inc(s[f"stored{par}"], 16)
            tiles(sp, body)
            for par in range(2):
                sp.wait_ge(s[f"stored{par}"], NT * 8 + 16)

        @block.scalar
        def _(act):
            act.sem_inc(s["tr_evac"], 1)

            def mix_stats(n, j, par):
                act.wait_ge(s[f"in{par}"], j * 112 + 112)
                act.wait_ge(s["mixed"], n + 1)
                nc.scalar.activation(junk[:, 1, :], o[par][:, :], ACT.Square).then_inc(s["sq_done"], 1)
                act.wait_ge(s["centred"], n + 1)
                nc.scalar.activation(junk[:, 0, :], yy[:, :], ACT.Square).then_inc(s["sq_done"], 1)
                act.wait_ge(s["var"], n + 1)
                nc.scalar.activation(st12[:, 2, :], st12[:, 1, :], ACT.Sqrt).then_inc(s["root"], 1)

            def evac(n, i, dst, bank, width=512):
                act.wait_ge(s["tr_ready"], n * 5 + i + 1)
                nc.scalar.copy(dst.rearrange("p k t -> p (k t)"), tr[bank][:, 0:width]).then_inc(s["tr_evac"], 1)

            def body(n, j, par, more):
                evac(n, 0, mixT[:, 0:4, :], 0)
                evac(n, 1, mixT[:, 4:8, :], 1)
                evac(n, 2, pT[:, :, :], 0, 256)
                act.wait_ge(s["e_mm"], n + 1)
                act.wait_ge(s["en_done"], n + 1)
                for i in range(2):
                    if i:
                        act.wait_ge(s["e_sq"], n * 2 + 1)
                    nc.scalar.activation(ejunk[:, :], eb[i][:, :], ACT.Square, accum_out=es[:, i:i + 1]).then_inc(s["e_sq"], 1)
                act.wait_ge(s["e_var"], n + 1)
                nc.scalar.activation(es[:, 3:4], es[:, 2:3], ACT.Sqrt).then_inc(s["e_root"], 1)
                evac(n, 3, hT[:, 0:4, :], 1)
                evac(n, 4, hT[:, 4:8, :], 0)
                if more:
                    mix_stats(n + 1, j + par, 1 - par)
                act.wait_ge(s["z_ready"], n + 2)
                nc.scalar.activation(zz[:, :], zz[:, :], ACT.Tanh, scale=0.5).then_inc(s["th_ready"], 1)

            mix_stats(0, 0, 0)
            tiles(act, body)

        @block.vector
        def _(dve):
            for n, c in (("mixed", 1), ("en_done", 1), ("z_ready", 1), ("h_ready", 0), ("stored0", 16), ("stored1", 16)):
                if c:
                    dve.sem_inc(s[n], c)
            dve.wait_ge(s["rows"], 5 * 16)
            nc.vector.tensor_scalar(subln[:, 0:P], subln[:, 0:P], 0.5 * (1.0 - LAM_INIT), None, ALU.mult).then_inc(s["scaled"], 1)
            dve.wait_ge(s["scaled"], 1)
            nc.vector.tensor_copy(subln[:, P:512].rearrange("p (h c) -> p h c", h=3), subln[:, 0:P].unsqueeze(1).broadcast_to([P, 3, P])).then_inc(s["scaled"], 1)
            dve.wait_ge(s["scaled"], 2)
            PER = 14

            def per_head(v, heads):
                return v.rearrange("p (h c) -> p h c", h=heads)

            def wide(v, heads):
                return v.unsqueeze(2).broadcast_to([P, heads, 512 // heads])

            def mixing(n, j, par):
                st = Steps(dve, s["step"], n * PER)
                tt, ts = nc.vector.tensor_tensor, nc.vector.tensor_scalar

                def then(ins):
                    st.step(ins)
                    st.settle()
                dve.wait_ge(s[f"in{par}"], j * 112 + 112)
                dve.wait_ge(s["mixed"], n + 1)
                then(tt(yy[:, :], yb[par][:, 0, :], yb[par][:, 1, :], ALU.add))
                then(nc.vector.tensor_reduce(st12[:, 0, 0:8], per_head(yy[:, :], 8), AX.X, ALU.add))
                then(ts(st12[:, 0, 0:8], st12[:, 0, 0:8], 1.0 / 64, None, ALU.mult))
                tt(per_head(yy[:, :], 8), per_head(yy[:, :], 8), wide(st12[:, 0, 0:8], 8), ALU.subtract).then_inc(s["centred"], 1)
                dve.wait_ge(s["sq_done"], n * 2 + 1)
                st.step(nc.vector.tensor_reduce(st12[:, 0, 8:12], per_head(junk[:, 1, :], 4), AX.X, ALU.add))
                dve.wait_ge(s["sq_done"], n * 2 + 2)
                then(nc.vector.tensor_reduce(st12[:, 0, 0:8], per_head(junk[:, 0, :], 8), AX.X, ALU.add))
                st.step(ts(st12[:, 1, 0:8], st12[:, 0, 0:8], 1.0 / 64, LN_EPS, ALU.mult, ALU.add))
                ts(st12[:, 1, 8:12], st12[:, 0, 8:12], 1.0 / P, NORM_EPS, ALU.mult, ALU.add).then_inc(s["var"], 1)
                dve.wait_ge(s["root"], n + 1)
                then(nc.vector.reciprocal(st12[:, 3, :], st12[:, 2, :]))
                st.step(tt(per_head(yy[:, :], 8), per_head(yy[:, :], 8), wide(st12[:, 3, 0:8], 8), ALU.mult))
                then(tt(per_head(o[par][:, :], 4), per_head(o[par][:, :], 4), wide(st12[:, 3, 8:12], 4), ALU.mult))
                st.step(tt(yy[:, :], yy[:, :], ln_g[:, :], ALU.mult))
                then(tt(o[par][:, :], o[par][:, :], subln[:, :], ALU.mult))
                st.step(tt(yy[:, :], yy[:, :], ln_b[:, :], ALU.add))
                then(tt(mix[:, 512:1024], o[par][:, :], gt[par][:, 1, :], ALU.mult))
                then(tt(yy[:, :], yy[:, :], bonus[par][:, :, :].rearrange("p g c -> p (g c)"), ALU.add))
                nc.vector.scalar_tensor_tensor(mix[:, 0:512], yy[:, :], 0.5, gt[par][:, 0, :], ALU.mult, ALU.mult).then_inc(s["mixed"], 1)
                return st

            def body(n, j, par, more):
                for i in range(2):
                    dve.wait_ge(s["h_mm"], n * 2 + i + 1)
                    c = slice(i * HALF, (i + 1) * HALF)
                    nc.vector.tensor_tensor(h[:, c], hb[i][:, :], x[par][:, c], ALU.add).then_inc(s["h_ready"], 1)
                dve.wait_ge(s["e_sq"], n * 2 + 2)
                nc.vector.tensor_scalar(es[:, 2:3], es[:, 0:1], es[:, 1:2], 1.0 / D_MODEL, ALU.add, ALU.mult).then_inc(s["tail"], 1)
                dve.wait_ge(s["tail"], n * 5 + 1)
                nc.vector.tensor_scalar(es[:, 2:3], es[:, 2:3], NORM_EPS, None, ALU.add).then_inc(s["e_var"], 1)
                dve.wait_ge(s["e_root"], n + 1)
                nc.vector.reciprocal(es[:, 4:5], es[:, 3:4]).then_inc(s["tail"], 1)
                dve.wait_ge(s["tail"], n * 5 + 2)
                for i in range(2):
                    c = slice(i * HALF, (i + 1) * HALF)
                    ins = nc.vector.scalar_tensor_tensor(en[:, c], eb[i][:, :], es[:, 4:5], ple_norm[:, c], ALU.mult, ALU.mult)
                    ins.then_inc(s["en_done" if i else "tail"], 1)
                if more:
                    mixing(n + 1, j + par, 1 - par)
                for i in range(2):
                    dve.wait_ge(s["g_mm"], n * 2 + i + 1)
                    c = slice(i * HALF, (i + 1) * HALF)
                    ins = nc.vector.tensor_tensor(zz[:, c], gb[i][:, :], gate_b[:, c], ALU.add)
                    ins.then_inc(s["z_ready" if i else "tail"], 1)
                dve.wait_ge(s["th_ready"], n + 1)
                dve.wait_ge(s["en_done"], n + 2)
                nc.vector.scalar_tensor_tensor(zz[:, :], zz[:, :], 1.0, en[:, :], ALU.add, ALU.mult).then_inc(s["tail"], 1)
                dve.wait_ge(s[f"stored{par}"], j * 16 + 16)
                dve.wait_ge(s["tail"], n * 5 + 5)
                nc.vector.scalar_tensor_tensor(out[par][:, :], zz[:, :], 0.5, h[:, :], ALU.mult, ALU.add).then_inc(s["out_ready"], 1)
                dve.wait_ge(s["out_ready"], n + 1)

            st = mixing(0, 0, 0)
            assert st.n == PER, st.n
            tiles(dve, body)

        @block.tensor
        def _(pe):
            pe.wait_ge(s["ident"], 16)

            def transposes(n, i, bank, before, sources):
                pe.wait_ge(s["tr_evac"], n * 5 + before + 1)
                for k, src in enumerate(sources):
                    last = nc.tensor.transpose(tr[bank][:, k * P:(k + 1) * P], src, ident[:, :])
                last.then_inc(s["tr_ready"], 1)

            def product(banks, lhsT, w, kc, signal, each=True):
                for i in range(2):
                    for k in range(kc):
                        last = nc.tensor.matmul(banks[i][:, :], lhsT[:, k, :], w[:, k, i * HALF:(i + 1) * HALF], start=(k == 0), stop=(k == kc - 1))
                    if each or i:
                        last.then_inc(s[signal], 1)

            def body(n, j, par, more):
                cols = [slice(k * P, (k + 1) * P) for k in range(KC)]
                pe.wait_ge(s["mixed"], n + 2)
                transposes(n, 0, 0, 0, [mix[:, c] for c in cols[0:4]])
                transposes(n, 1, 1, 0, [mix[:, c] for c in cols[4:8]])
                pe.wait_ge(s[f"in{par}"], j * 112 + 112)
                transposes(n, 2, 0, 1, [p[par][:, c] for c in cols[0:2]])
                pe.wait_ge(s["wo"], 16)
                pe.wait_ge(s["tr_evac"], n * 5 + 3)
                product(hb, mixT, wo, KC, "h_mm")
                pe.wait_ge(s["wp"], 16)
                pe.wait_ge(s["en_done"], n + 1)
                pe.wait_ge(s["tr_evac"], n * 5 + 4)
                product(eb, pT, wp, 2, "e_mm", each=False)
                pe.wait_ge(s["h_ready"], n * 2 + 1)
                transposes(n, 3, 1, 2, [h[:, c] for c in cols[0:4]])
                pe.wait_ge(s["h_ready"], n * 2 + 2)
                transposes(n, 4, 0, 3, [h[:, c] for c in cols[4:8]])
                pe.wait_ge(s["wg"], 16)
                pe.wait_ge(s["z_ready"], n + 1)
                pe.wait_ge(s["tr_evac"], n * 5 + 6)
                product(gb, hT, wg, KC, "g_mm")
            tiles(pe, body)
PARAMS = ["x", "p", "norm_pre", "w_in", "w_out", "rw_conv_w", "rw_conv_b", "rw_w0", "rw_w_up", "rw_a0", "rw_a_up", "rw_k_k",
          "rw_k_a", "rw_r_k", "rw_ln_g", "rw_ln_b", "da_q_norm", "da_k_norm", "da_lambda", "da_subln", "ple_proj", "ple_norm",
          "ple_gate_w", "ple_gate_b", "ident"]


def hybrid_encoder(nc, a, out, sequences):
    tokens = a["x"].shape[0]
    G = RW_WIDTH // P
    NI = G * (tokens // P)

    def scratch(name, shape):
        return nc.dram_tensor(f"scratch_{name}", shape, F32).ap()
    conv_in = scratch("conv_in", (14 * P, tokens + 2))
    q_kT = scratch("q_kT", (2 * DA_WIDTH, tokens))
    v_tok = scratch("v_tok", (tokens, DA_WIDTH))
    gates = [scratch(f"gate{i}", (tokens, 512)) for i in range(2)]
    packs = scratch("packs", (NI, P, PK_END))
    carry = scratch("carry", (NI, P, 2, 256))
    local = scratch("local", (NI, P, 3, P))
    y = scratch("y", (2, tokens, RW_WIDTH))
    o_tok = scratch("o_tok", (tokens, DA_WIDTH))

    with ExitStack() as ctx:
        table = ctx.enter_context(nc.sbuf_tensor("table", [P, T_END], F32))
        project_phase(nc, tokens, a["x"].rearrange("(b t p) d -> b p t d", t=2, p=P), a["norm_pre"], a["w_in"][0],
                      a["da_q_norm"], a["da_k_norm"], a["ident"], conv_in, q_kT, v_tok, gates)
        prepare_phase(nc, tokens, conv_in, packs, a["rw_w_up"], a["rw_a_up"], a["ident"],
                      [a[n] for n in ("rw_conv_w", "rw_conv_b", "rw_w0", "rw_a0", "rw_k_k", "rw_k_a", "rw_r_k")], table)
        unit_phase(nc, tokens, packs, carry, local, a["ident"], table)
        chain_phase(nc, tokens, sequences, carry, local, y)
        for i, (first, count) in enumerate(sequences):
            attention_phase(nc, f"at{i}", first, count, q_kT, v_tok, o_tok, a["da_lambda"], a["ident"])
        output_phase(nc, tokens, a["x"].rearrange("(c p) d -> c p d", p=P), a["p"].rearrange("(c p) d -> c p d", p=P), y, local, gates,
                     o_tok, out.rearrange("(c p) d -> c p d", p=P), a["w_out"][0], a["ple_proj"][0], a["ple_gate_w"][0],
                     [a[n] for n in ("rw_ln_g", "rw_ln_b", "da_subln", "ple_norm", "ple_gate_b")], a["ident"])


def kernel(**inputs):
    import numpy as np
    import concourse.bacc as bacc
    from concourse.bass_utils import run_bass_kernel_spmd

    nc = bacc.Bacc("TRN2", target_bir_lowering=False, num_devices=1)
    lengths = [inputs["x_prompt"].shape[1], inputs["x_sample"].shape[1]]
    arrays = {n: np.ascontiguousarray(inputs[n]) for n in PARAMS if n in inputs}
    arrays["x"] = np.concatenate([np.asarray(inputs["x_prompt"])[0], np.asarray(inputs["x_sample"])[0]])
    arrays["p"] = np.concatenate([np.asarray(inputs["p_prompt"])[0, 0], np.asarray(inputs["p_sample"])[0, 0]])
    arrays["ident"] = np.eye(P, dtype=np.float32)
    maps = {f"in_{n}_dram": arrays[n] for n in PARAMS}
    a = {n: nc.dram_tensor(f"in_{n}_dram", arrays[n].shape, mybir.dt.from_np(arrays[n].dtype), kind="ExternalInput").ap() for n in PARAMS}
    out = nc.dram_tensor("out_dram", (sum(lengths), D_MODEL), F32, kind="ExternalOutput").ap()
    chunks = [n // P for n in lengths]
    hybrid_encoder(nc, a, out, [(0, chunks[0]), (chunks[0], chunks[1])])
    r = run_bass_kernel_spmd(nc, [maps], core_ids=[0])
    got = r.results[0]["out_dram"]
    return got[None, 0:lengths[0]], got[None, lengths[0]:]
```
